# Optimizing a Trainium2 kernel written in Bass

```python
import jax, jax.numpy as jnp
from jax import lax
import numpy as np

D_MODEL = 1024
BATCH = 1
SEQ = 4096
DEPTH = 1

D_MIX = D_MODEL
D_POOL = D_MIX // 2
D_MLSTM = D_MIX - D_POOL
POOL_WINDOWS = (2, 4, 8, 16)
N_POOL_GROUPS = len(POOL_WINDOWS)
POOL_GROUP_DIM = D_POOL // N_POOL_GROUPS
N_HEADS = 4
HEAD_DIM = D_MLSTM // N_HEADS
CONV_WIDTH = 4
CHUNK = 128
EPS = 1e-6
OFF_U = 0
OFF_ZP = OFF_U + D_POOL
OFF_Q = OFF_ZP + D_POOL
OFF_K = OFF_Q + D_MLSTM
OFF_V = OFF_K + D_MLSTM
OFF_O = OFF_V + D_MLSTM
OFF_ZM = OFF_O + D_MLSTM
OFF_G = OFF_ZM + D_MLSTM
D_IN_PROJ = OFF_G + 2 * N_HEADS

kernel_name = "hymba_pool_mlstm_adaln_block"

def rms_norm(x, g):
    xf = x.astype(jnp.float32)
    y = xf * lax.rsqrt(jnp.mean(xf * xf, axis=-1, keepdims=True) + EPS)
    return (y * g.astype(jnp.float32)).astype(x.dtype)

def causal_pool_mixer(u, w_pool, ls_pool):
    B, S, _ = u.shape
    ug = u.astype(jnp.float32).reshape(B, S, N_POOL_GROUPS, POOL_GROUP_DIM)
    cs = jnp.cumsum(ug, axis=1)
    pos = jnp.arange(1, S + 1, dtype=jnp.float32)
    outs = []
    for g, w in enumerate(POOL_WINDOWS):
        c_g = cs[:, :, g]
        lag = jnp.pad(c_g[:, :S - w], ((0, 0), (w, 0), (0, 0)))
        mean = (c_g - lag) / jnp.minimum(pos, float(w))[None, :, None]
        outs.append(mean - ug[:, :, g])
    pooled = jnp.stack(outs, axis=2)
    y = jnp.einsum('bsgc,gcd->bsgd', pooled, w_pool.astype(jnp.float32))
    y = y.reshape(B, S, D_POOL) * ls_pool.astype(jnp.float32)
    return y.astype(u.dtype)

def causal_depthwise_conv(x, w, b):
    S = x.shape[1]
    xp = jnp.pad(x, ((0, 0), (CONV_WIDTH - 1, 0), (0, 0)))
    y = b
    for j in range(CONV_WIDTH):
        y = y + w[j] * xp[:, j:j + S]
    return y

def _mlstm_chunk_step(carry, inp):
    C, n, m = carry
    q, k, v, ig, lf = inp
    L = q.shape[2]
    b = jnp.cumsum(lf, axis=-1)
    causal = jnp.tril(jnp.ones((L, L), dtype=bool))
    d_log = jnp.where(causal, b[..., :, None] - b[..., None, :] + ig[..., None, :], -jnp.inf)
    inter_log = b + m[..., None]
    m_t = jnp.maximum(inter_log, jnp.max(d_log, axis=-1))
    dmat = jnp.exp(d_log - m_t[..., None])
    inter = jnp.exp(inter_log - m_t)
    s = jnp.einsum('bhtd,bhsd->bhts', q, k) * dmat
    num = jnp.einsum('bhts,bhsd->bhtd', s, v) + inter[..., None] * jnp.einsum('bhvd,bhtd->bhtv', C, q)
    den = jnp.sum(s, axis=-1) + inter * jnp.einsum('bhd,bhtd->bht', n, q)
    h = num / jnp.maximum(jnp.abs(den), jnp.exp(-m_t))[..., None]
    b_last = b[..., -1]
    w_log = b_last[..., None] - b + ig
    m_new = jnp.maximum(b_last + m, jnp.max(w_log, axis=-1))
    w = jnp.exp(w_log - m_new[..., None])
    decay = jnp.exp(b_last + m - m_new)
    C_new = decay[..., None, None] * C + jnp.einsum('bhs,bhsv,bhsd->bhvd', w, v, k)
    n_new = decay[..., None] * n + jnp.einsum('bhs,bhsd->bhd', w, k)
    return (C_new, n_new, m_new), h

def _to_chunks(a):
    B, S = a.shape[:2]
    a = a.reshape((B, S // CHUNK, CHUNK) + a.shape[2:])
    return jnp.swapaxes(jnp.moveaxis(a, 1, 0), 2, 3)

def mlstm_chunkwise(q, k, v, ig, lf):
    B, S, H, dh = q.shape
    f32 = jnp.float32
    k = k / jnp.sqrt(jnp.asarray(dh, f32)).astype(k.dtype)
    xs = tuple(_to_chunks(a.astype(f32)) for a in (q, k, v, ig, lf))
    carry0 = (jnp.zeros((B, H, dh, dh), f32), jnp.zeros((B, H, dh), f32), jnp.zeros((B, H), f32))
    _, hs = lax.scan(_mlstm_chunk_step, carry0, xs)
    hs = jnp.moveaxis(jnp.swapaxes(hs, 2, 3), 0, 1)
    return hs.reshape(B, S, H, dh)

def setup_inputs(seed: int = 0) -> dict:
    key = jax.random.key(seed)
    ks = jax.random.split(key, 16)
    nrm = jax.random.normal
    f32 = jnp.float32
    x = nrm(ks[0], (BATCH, SEQ, D_MODEL), f32)
    c = nrm(ks[1], (BATCH, D_MODEL), f32)
    norm_g = 1.0 + 0.02 * nrm(ks[2], (DEPTH, D_MODEL), f32)
    w_ada = 0.5 * D_MODEL ** -0.5 * nrm(ks[3], (DEPTH, D_MODEL, 3 * D_MODEL), f32)
    b_ada = 0.01 * nrm(ks[4], (DEPTH, 3 * D_MODEL), f32)
    w_in = D_MODEL ** -0.5 * nrm(ks[5], (DEPTH, D_MODEL, D_IN_PROJ), f32)
    b_igate = 0.1 * nrm(ks[6], (DEPTH, N_HEADS), f32)
    b_fgate = jnp.linspace(3.0, 6.0, N_HEADS, dtype=f32)[None, :] + 0.1 * nrm(ks[7], (DEPTH, N_HEADS), f32)
    b_gates = jnp.concatenate([b_igate, b_fgate], axis=-1)
    conv_w = 0.5 * nrm(ks[8], (DEPTH, CONV_WIDTH, 2 * D_MLSTM), f32)
    conv_b = 0.02 * nrm(ks[9], (DEPTH, 2 * D_MLSTM), f32)
    w_pool = POOL_GROUP_DIM ** -0.5 * nrm(ks[10], (DEPTH, N_POOL_GROUPS, POOL_GROUP_DIM, POOL_GROUP_DIM), f32)
    ls_pool = 1.0 + 0.1 * nrm(ks[11], (DEPTH, D_POOL), f32)
    mh_norm_g = 1.0 + 0.02 * nrm(ks[12], (DEPTH, D_MLSTM), f32)
    w_out = D_MIX ** -0.5 * nrm(ks[13], (DEPTH, D_MIX, D_MODEL), f32)
    final_g = 1.0 + 0.02 * nrm(ks[14], (D_MODEL,), f32)
    return {"x": x, "c": c, "norm_g": norm_g, "w_ada": w_ada, "b_ada": b_ada,
            "w_in": w_in, "b_gates": b_gates, "conv_w": conv_w, "conv_b": conv_b,
            "w_pool": w_pool, "ls_pool": ls_pool, "mh_norm_g": mh_norm_g,
            "w_out": w_out, "final_g": final_g}

def reference(x, c, norm_g, w_ada, b_ada, w_in, b_gates, conv_w, conv_b,
              w_pool, ls_pool, mh_norm_g, w_out, final_g):
    B, S, _ = x.shape
    for l in range(DEPTH):
        mod = jax.nn.silu(c) @ w_ada[l] + b_ada[l]
        shift, scale, gate = jnp.split(mod, 3, axis=-1)
        h = rms_norm(x, norm_g[l]) * (1.0 + scale[:, None, :]) + shift[:, None, :]
        proj = h @ w_in[l]

        u = proj[..., OFF_U:OFF_ZP]
        z_pool = proj[..., OFF_ZP:OFF_Q]
        pool_out = causal_pool_mixer(u, w_pool[l], ls_pool[l]) * jax.nn.silu(z_pool)

        qk = jax.nn.silu(causal_depthwise_conv(proj[..., OFF_Q:OFF_V], conv_w[l], conv_b[l]))
        q = qk[..., :D_MLSTM].reshape(B, S, N_HEADS, HEAD_DIM)
        k = qk[..., D_MLSTM:].reshape(B, S, N_HEADS, HEAD_DIM)
        v = proj[..., OFF_V:OFF_O].reshape(B, S, N_HEADS, HEAD_DIM)
        o_gate = jax.nn.sigmoid(proj[..., OFF_O:OFF_ZM])
        z_mlstm = proj[..., OFF_ZM:OFF_G]
        gates = (proj[..., OFF_G:] + b_gates[l]).astype(jnp.float32)
        ig = gates[..., :N_HEADS]
        lf = jax.nn.log_sigmoid(gates[..., N_HEADS:])
        hm = mlstm_chunkwise(q, k, v, ig, lf)
        hm = hm * lax.rsqrt(jnp.mean(hm * hm, axis=-1, keepdims=True) + EPS)
        hm = hm.reshape(B, S, D_MLSTM) * mh_norm_g[l].astype(jnp.float32)
        mlstm_out = hm.astype(x.dtype) * o_gate * jax.nn.silu(z_mlstm)

        mix = jnp.concatenate([pool_out, mlstm_out], axis=-1)
        x = x + gate[:, None, :] * (mix @ w_out[l])
    return rms_norm(x, final_g)


_drawn_inputs = setup_inputs


def setup_inputs(seed=0):
    import zlib

    import numpy as np

    out = dict(_drawn_inputs(seed))
    spreads = {}
    factors = {'norm_g': 8.0,
     'b_ada': 8.0,
     'conv_b': 64.0,
     'ls_pool': 3.945,
     'mh_norm_g': 64.0,
     'final_g': 8.827,
     'conv_w': 3.968}
    for name, (base, spread) in spreads.items():
        noise = np.random.default_rng([zlib.crc32(name.encode()), seed]).standard_normal(out[name].shape)
        drawn = base * np.exp(spread * noise) if base else spread * noise
        out[name] = __import__('jax').numpy.asarray(drawn.astype(out[name].dtype))
    for name, factor in factors.items():
        out[name] = (out[name] * factor).astype(out[name].dtype)
    return out
```

```python
from contextlib import ExitStack

import numpy as np

import concourse.bass as bass
from concourse import mybir

F32 = mybir.dt.float32
F32R = mybir.dt.float32r
BF16 = mybir.dt.bfloat16
ALU = mybir.AluOpType
ACT = mybir.ActivationFunctionType
AX = mybir.AxisListType

P = 128
D = 1024
KT = D // P
SEQ = 4096
BLK = 512
NB = SEQ // BLK
NC = BLK // P
NH = 4
CW = 4
WINDOWS = (2, 4, 8, 16)
EPS = 1e-6
OFF_U, OFF_ZP, OFF_Q, OFF_K, OFF_V, OFF_O, OFF_ZM, OFF_G = (512 * i for i in range(8))
QK_SCALE = 1.0 / (4.0 * float(np.sqrt(float(P))))
BIG = 1e38
HALO = 16

RING = 4
V_UNITS = KT
UNITS = V_UNITS + 2 * 24
WU = UNITS // RING
TASKS = 36
TANHS = 20
SCO_FULLS = 8
S_USES = 1 + SCO_FULLS
B_USES = 12
PREPS = 8
DVE_STEPS = 87
C_NG, C_C, C_BA, C_CW, C_CB, C_LS, C_MG, C_END = 0, 8, 16, 40, 72, 80, 84, 88
K_ID, K_TRI, K_BIG, K_END = 0, 128, 256, 384
K_COR = 15 * NH

TASK = {}
for _i in range(4):
    TASK["q", _i], TASK["k", _i], TASK["z", _i], TASK["o", _i] = _i, 4 + _i, 8 + _i, 12 + _i
TASK["u", 0], TASK["zp", 0] = 16, 17
for _i in range(1, 4):
    TASK["u", _i], TASK["y", _i - 1], TASK["zp", _i] = 15 + 3 * _i, 16 + 3 * _i, 17 + 3 * _i
TASK["y", 3] = 27
for _i in range(8):
    TASK["out", _i] = 28 + _i
SCO = {("qk", 0): 1, ("qk", 1): 2, ("hm", 0): 3, ("qk", 2): 4, ("hm", 1): 5, ("qk", 3): 6, ("hm", 2): 7, ("hm", 3): 8}
TILES = [(n, i) for n in ("q", "k", "z", "o") for i in range(4)] + [(n, i) for i in range(4) for n in ("u", "zp")]
TANH_TILES = TILES[:16] + [("zp", i) for i in range(4)]
OFFSET = {"q": OFF_Q, "k": OFF_K, "z": OFF_ZM, "o": OFF_O, "u": OFF_U, "zp": OFF_ZP}


def unit0(name, i):
    return V_UNITS + 2 * TILES.index((name, i))


def build(nc, x, c, norm_g, w_ada, b_ada, w_in, b_gates, conv_w, conv_b, w_pool, ls_pool, mh_norm_g,
          w_out, final_g, consts, out):
    with ExitStack() as ctx:
        def sb(name, shape, dt=F32):
            return ctx.enter_context(nc.sbuf_tensor("sb_" + name, shape, dt))

        def bank(name):
            return ctx.enter_context(nc.psum_tensor("ps_" + name, [P, 512], F32))

        def sem(name):
            return ctx.enter_context(nc.semaphore(name))

        hT_hi, hT_lo = sb("hT_hi", [P, KT, BLK], F32R), sb("hT_lo", [P, KT, BLK], F32R)
        wo_hi, wo_lo = sb("wo_hi", [P, KT, D], F32R), sb("wo_lo", [P, KT, D], F32R)
        w_raw = sb("w_raw", [P, RING, 512])
        w_hi, w_lo = sb("w_hi", [P, RING, 512], F32R), sb("w_lo", [P, RING, 512], F32R)
        wg_raw = sb("wg_raw", [P, KT, 8])
        wg_hi, wg_lo = sb("wg_hi", [P, KT, 8], F32R), sb("wg_lo", [P, KT, 8], F32R)
        qT, kT, oz = sb("qT", [P, NH, BLK]), sb("kT", [P, NH, BLK]), sb("oz", [P, NH, BLK])
        v = sb("v", [P, NC, NH, P + 1])
        mixp_hi, mixp_lo = sb("mixp_hi", [P, NH, BLK], F32R), sb("mixp_lo", [P, NH, BLK], F32R)
        mixm_hi, mixm_lo = sb("mixm_hi", [P, 2, NH, P], F32R), sb("mixm_lo", [P, 2, NH, P], F32R)
        shifted = sb("shifted", [P, 2, HALO + BLK])
        acc_cv = sb("acc_cv", [P, HALO + BLK])
        tanh = sb("tanh", [P, BLK])
        halo_qk, halo_u = sb("halo_qk", [P, 8, CW - 1]), sb("halo_u", [P, NH, HALO])
        silu_zp = sb("silu_zp", [P, BLK])
        dmat = sb("dmat", [P, NH, P])
        q_in = sb("q_in", [P, NH, P])
        k_w = sb("k_w", [P, NH, P])
        hm = q_in
        cmem = sb("cmem", [P, NH, P + 1])
        x_in = sb("x_in", [P, 2, D])
        x_res = sb("x_res", [P, 2, D])
        full = [dmat, k_w]
        junk = tanh[:, :].bitcast(BF16)
        fg = sb("fg", [P, D])
        wpool = sb("wpool", [P, NH, P])
        cst = sb("cst", [P, K_END])
        warm = sb("warm", [P, NH, 15])
        par = sb("par", [P, C_END])
        gain, shift = sb("gain", [P, KT]), sb("shift", [P, KT])
        gate_col = sb("gate_col", [P, KT])
        silu_c = sb("silu_c", [P, KT])
        mg4, ls2 = sb("mg4", [P, NH]), sb("ls2", [P, NH])
        bg = sb("bg", [P, 8])
        ones = sb("ones", [P, 1])
        g_pre = sb("g_pre", [P, NC, 8])
        g_abs, g_e, lf = sb("g_abs", [P, 16]), sb("g_e", [P, 16]), sb("lf", [P, 16])
        b_cum = sb("b_cum", [P, 32])
        a_pad = sb("a_pad", [P, P])
        aT, cmax, mp_diag = silu_zp[0:16, 0:P], silu_zp[0:16, P:2 * P], silu_zp[0:16, 2 * P:2 * P + 16]
        diag = sb("diag", [P, 16])
        m_prev, m_last = sb("m_prev", [P, 20]), sb("m_last", [P, 16])
        mp_col = sb("mp_col", [16, 1])
        m_row, inter_row = sb("m_row", [P, P]), sb("inter_row", [P, P])
        expo = sb("expo", [P, 3, 16])
        den, rden = sb("den", [P, NH]), sb("rden", [P, NH])
        h_sq, h_var, h_rs = sb("h_sq", [P, NH]), sb("h_var", [P, NH]), sb("h_rs", [P, NH])
        x_sq, x_var, x_rs = sb("x_sq", [P, 2]), sb("x_var", [P, 2]), sb("x_rs", [P, 2])
        o_sq, o_var, o_rs = sb("o_sq", [P, 2]), sb("o_var", [P, 2]), sb("o_rs", [P, 2])
        mhalf = sb("mhalf", [P, NH])

        acc = [bank("acc0"), bank("acc1")]
        sco = bank("sco")
        bro = bank("bro")
        num = [bank("num0"), bank("num1")]
        kv = [bank("kv0"), bank("kv1")]
        v_bank = [num[0], num[1], kv[0], kv[1]]

        ident, tri, bigm = cst[:, K_ID:K_ID + P], cst[:, K_TRI:K_TRI + P], cst[:, K_BIG:K_BIG + P]

        cst_loaded, par_loaded, misc_loaded = sem("cst_loaded"), sem("par_loaded"), sem("misc_loaded")
        rows_zeroed, mhalf_ready = sem("rows_zeroed"), sem("mhalf_ready")
        fg_loaded, wg_loaded = sem("fg_loaded"), sem("wg_loaded")
        ada_loaded = [sem(f"ada_loaded{i}") for i in range(3)]
        ada_used = sem("ada_used")
        wout_loaded = [sem(f"wout_loaded{i}") for i in range(2)]
        wout_scaled, wout_hi_done, wout_lo_done = sem("wout_scaled"), sem("wout_hi_done"), sem("wout_lo_done")
        w_loaded = [sem(f"w_loaded{i}") for i in range(RING)]
        w_hi_done, w_lo_done, w_used = sem("w_hi_done"), sem("w_lo_done"), sem("w_used")
        wg_hi_done, wg_lo_done = sem("wg_hi_done"), sem("wg_lo_done")
        par_T, par_ready, c_tanh, silu_c_ready = sem("par_T"), sem("par_ready"), sem("c_tanh"), sem("silu_c_ready")
        mod_done, gate_done, gate_ready, gate_bc = sem("mod_done"), sem("gate_done"), sem("gate_ready"), sem("gate_bc")
        setup_done = sem("setup_done")
        x_loaded = [sem("x_loaded0"), sem("x_loaded1")]
        x_sq_done, x_var_done, x_rs_done, x_scaled = sem("x_sq_done"), sem("x_var_done"), sem("x_rs_done"), sem("x_scaled")
        x_T, h_full, h_hi, h_lo = sem("x_T"), sem("h_full"), sem("h_hi"), sem("h_lo")
        gates_done, gates_T, g_rows_ready, g_abs_done, g_ln_done, lf_ready = sem("gates_done"), sem("gates_T"), sem("g_rows_ready"), sem("g_abs_done"), sem("g_ln_done"), sem("lf_ready")
        g_exp_done = sem("g_exp_done")
        a_ready, diag_ready, m_ready = sem("a_ready"), sem("diag_ready"), sem("m_ready")
        inter_row_ready, expo_ready, expo_done = sem("inter_row_ready"), sem("expo_ready"), sem("expo_done")
        bro_full, bro_free = sem("bro_full"), sem("bro_free")
        sco_full, sco_free = sem("sco_full"), sem("sco_free")
        acc_full = sem("acc_full")
        acc_free = [sem("acc_free0"), sem("acc_free1")]
        v_done, v_copied_act, v_copied_dve = sem("v_done"), sem("v_copied_act"), sem("v_copied_dve")
        shifted_free, conv_done = sem("shifted_free"), sem("conv_done")
        tanh_ready, qk_ready, o_tanh = sem("tanh_ready"), sem("qk_ready"), sem("o_tanh")
        pooled_ready, k_T, d_exp, k_w_ready = sem("pooled_ready"), sem("k_T"), sem("d_exp"), sem("k_w_ready")
        num_done, kv_done, h_ready, c_done = sem("num_done"), sem("kv_done"), sem("h_ready"), sem("c_done")
        h_sq_done, h_var_done, h_rs_done, hm_ready = sem("h_sq_done"), sem("h_var_done"), sem("h_rs_done"), sem("hm_ready")
        y_hi, y_lo, m_hi, m_lo = sem("y_hi"), sem("y_lo"), sem("m_hi"), sem("m_lo")
        res_loaded = [sem("res_loaded0"), sem("res_loaded1")]
        stored = [sem("stored0"), sem("stored1")]
        o_sq_done, o_var_done, o_rs_done, o_ready = (
            sem("o_sq_done"), sem("o_var_done"), sem("o_rs_done"), sem("o_ready"))
        dve_step = sem("dve_step")

        block = ctx.enter_context(nc.Block())

        w_in_v = w_in[0].rearrange("(k p) n -> p k n", p=P)
        w_ada_v = w_ada[0].rearrange("(k p) n -> p k n", p=P)
        ada_buf = [t[:, :, :].rearrange("p h (a n) -> p (h a) n", n=256) for t in (qT, kT, oz)]

        def reach(eng, sem, value):
            if not (isinstance(value, int) and value <= 0):
                eng.wait_ge(sem, value)

        def chunk(j):
            return slice(P * j, P * j + P)

        def col(t, n, m=P):
            return t[:, n:n + 1].broadcast_to([P, m])

        @block.sync
        def _(sp):
            def load_w(b, m):
                if m >= RING or b is not None:
                    sp.wait_ge(w_lo_done, m - RING + 1 if b is None else b * UNITS + (m - RING + 1))
                n = m % UNITS
                if n < V_UNITS:
                    src, dst = w_in_v[:, n, OFF_V:OFF_V + 512], w_raw[:, m % RING, :]
                else:
                    name, i = TILES[(n - V_UNITS) // 2]
                    half = (n - V_UNITS) % 2
                    off = OFFSET[name] + P * i
                    src = w_in_v[:, 4 * half:4 * half + 4, off:off + P]
                    dst = w_raw[:, m % RING, :].rearrange("p (k n) -> p k n", n=P)
                sp.dma_start(dst, src).then_inc(w_loaded[m % RING], 16)

            def load_x(nb, c, first=False):
                if not first:
                    sp.wait_ge(x_T, nb * PREPS + (2 * c - 2))
                sp.dma_start(x_in[:, c % 2, :], x[0, bass.ds(nb * BLK + c * P, P), :]).then_inc(x_loaded[c % 2], 16)

            def load_res(b, j):
                reach(sp, stored[j % 2], 16 * (b * 2 + j // 2))
                sp.dma_start(x_res[:, j % 2, :], x[0, bass.ds(b * BLK + j * P, P), :]).then_inc(res_loaded[j % 2], 16)

            def store(b, j):
                sp.wait_ge(o_ready, b * NC + (j + 1))
                sp.dma_start(out[0, bass.ds(b * BLK + j * P, P), :], x_res[:, j % 2, :]).then_inc(stored[j % 2], 16)

            sp.dma_start(cst[:, :], consts[:, 0:K_END]).then_inc(cst_loaded, 16)
            sp.dma_start(warm[:, :, :].rearrange("p g n -> p (g n)"), consts[:, K_END:K_END + K_COR]).then_inc(misc_loaded, 16)
            rows = x_res[:, 0, 0:P]
            sp.wait_ge(rows_zeroed, 1)
            for at, src in ((C_NG, norm_g[0].rearrange("(t p) -> t p", p=P)), (C_C, c[0].rearrange("(t p) -> t p", p=P)),
                            (C_BA, b_ada[0].rearrange("(t p) -> t p", p=P)),
                            (C_CW, conv_w[0].rearrange("j (t p) -> (j t) p", p=P)),
                            (C_CB, conv_b[0].rearrange("(t p) -> t p", p=P)),
                            (C_LS, ls_pool[0].rearrange("(t p) -> t p", p=P)),
                            (C_MG, mh_norm_g[0].rearrange("(t p) -> t p", p=P))):
                sp.dma_start(rows[at:at + src.shape[0], :], src).then_inc(par_loaded, 16)

            def load_ada(g):
                if g >= 3:
                    sp.wait_ge(ada_used, g - 2)
                sp.dma_start(ada_buf[g % 3], w_ada_v[:, :, 256 * g:256 * g + 256]).then_inc(ada_loaded[g % 3], 16)

            for g in range(3):
                load_ada(g)
            load_x(0, 0, True)
            load_x(0, 1, True)
            for g in range(3, 8):
                load_ada(g)
            sp.dma_start(wg_raw[:, :, :], w_in_v[:, :, OFF_G:OFF_G + 8]).then_inc(wg_loaded, 16)
            sp.dma_start(bg[:, :], b_gates[0].partition_broadcast(P)).then_inc(misc_loaded, 16)
            for m in range(4):
                load_w(None, m)
            for g in range(8, 11):
                load_ada(g)
            sp.dma_start(wpool[:, :, :], w_pool[0].rearrange("g c d -> c g d")).then_inc(misc_loaded, 16)
            sp.dma_start(fg[:, :], final_g.partition_broadcast(P)).then_inc(fg_loaded, 16)
            load_x(0, 2)
            load_x(0, 3)
            load_ada(11)
            sp.wait_ge(par_ready, 1)
            for k in range(KT):
                if k >= 2:
                    sp.wait_ge(wout_lo_done, k - 1)
                sp.dma_start(x_res[:, k % 2, :], w_out[0, P * k:P * k + P, :]).then_inc(wout_loaded[k % 2], 16)
            for m in range(4, 8):
                load_w(None, m)
            sp.wait_ge(wout_lo_done, KT)

            def one_block(b, last):
                for m in range(8, UNITS):
                    load_w(b, m)
                    if m == 40 and not last:
                        load_x(b + 1, 0)
                        load_x(b + 1, 1)
                    if m == 48:
                        load_res(b, 0)
                        load_res(b, 1)
                if not last:
                    for m in range(UNITS, UNITS + 4):
                        load_w(b, m)
                    load_x(b + 1, 2)
                store(b, 0)
                if not last:
                    load_w(b, UNITS + 4)
                    load_w(b, UNITS + 5)
                    load_x(b + 1, 3)
                load_res(b, 2)
                store(b, 1)
                load_res(b, 3)
                if not last:
                    load_w(b, UNITS + 6)
                    load_w(b, UNITS + 7)
                store(b, 2)
                store(b, 3)

            one_block(0, False)
            with sp.Fori(1, NB - 1) as b:
                one_block(b, False)
            one_block(NB - 1, True)
            for i in range(2):
                sp.wait_ge(stored[i], 16 * 2 * NB)

        @block.tensor
        def _(pe):
            def split3(dst, st_hi, st_lo, mv_hi, mv_lo, start, stop):
                pe.matmul(dst, st_hi, mv_hi, start=start, stop=False)
                pe.matmul(dst, st_hi, mv_lo, start=False, stop=False)
                return pe.matmul(dst, st_lo, mv_hi, start=False, stop=stop)

            def prep(nb, p):
                c, half = p // 2, p % 2
                if half == 0:
                    pe.wait_ge(x_scaled, nb * NC + (c + 1))
                if p >= 2:
                    pe.wait_ge(h_full, nb * PREPS + (p - 1))
                for i in range(4):
                    k = 4 * half + i
                    last = pe.transpose(num[p % 2][:, chunk(i)], x_in[:, c % 2, chunk(k)], ident)
                last.then_inc(x_T, 1)

            pe.wait_ge(cst_loaded, 16)
            pe.wait_ge(par_loaded, 16 * 7)
            pe.transpose(kv[0][:, 0:P], x_res[:, 0, 0:P], ident).then_inc(par_T, 1)
            pe.wait_ge(silu_c_ready, 1)

            def ada(g):
                pe.wait_ge(ada_loaded[g % 3], 16 * (g // 3 + 1))
                for t in range(2 * g, 2 * g + 2):
                    dst = kv[1][:, t:t + 1] if t < 16 else sco[:, t:t + 1]
                    for k in range(KT):
                        last = pe.matmul(dst, ada_buf[g % 3][:, k, P * (t % 2):P * (t % 2) + P], silu_c[:, k:k + 1],
                                         start=(k == 0), stop=(k == KT - 1))
                return last.then_inc(ada_used, 1)

            for g in range(8):
                ada(g)
            for p in range(PREPS):
                prep(0, p)
            for g in range(8, 12):
                ada(g)
            pe.wait_ge(gate_ready, 1)
            for n in range(KT):
                last = pe.matmul(kv[n // 4][:, chunk(n % 4)], col(gate_col, n), ident, start=True, stop=True)
            last.then_inc(gate_bc, 1)
            pe.wait_ge(wout_scaled, KT)
            pe.wait_ge(setup_done, 1)

            def one_block(b, last_block):
                def acc_wait(name, i):
                    t = TASK[name, i]
                    reach(pe, acc_free[t % 2], b * (TASKS // 2) + t // 2)
                    return acc[t % 2]

                def tile(name, i):
                    dst = acc_wait(name, i)
                    for half in range(2):
                        m = unit0(name, i) + half
                        pe.wait_ge(w_lo_done, b * UNITS + (m + 1))
                        for k in range(4):
                            kk = 4 * half + k
                            last = split3(dst[:, :], w_hi[:, m % RING, chunk(k)], w_lo[:, m % RING, chunk(k)],
                                          hT_hi[:, kk, :], hT_lo[:, kk, :], kk == 0, kk == KT - 1)
                        if half == 0:
                            last.then_inc(w_used, 1)
                        else:
                            last.then_inc(acc_full, 1)

                def bro_wait(u):
                    reach(pe, bro_free, b * B_USES + u)

                pe.wait_ge(h_lo, b * PREPS + PREPS)
                pe.wait_ge(wg_lo_done, 1)
                reach(pe, sco_free, b * S_USES)
                for k in range(KT):
                    last = split3(sco[0:8, :], wg_hi[:, k, :], wg_lo[:, k, :], hT_hi[:, k, :], hT_lo[:, k, :],
                                  k == 0, k == KT - 1)
                last.then_inc(gates_done, 1)
                pe.wait_ge(h_full, b * PREPS + PREPS)
                reach(pe, c_done, b * NC)
                for k in range(V_UNITS):
                    pe.wait_ge(w_lo_done, b * UNITS + (k + 1))
                    for j in range(NC):
                        last = split3(v_bank[j][:, :], hT_hi[:, k, chunk(j)], hT_lo[:, k, chunk(j)],
                                      w_hi[:, k % RING, :], w_lo[:, k % RING, :], k == 0, k == KT - 1)
                    last.then_inc(w_used if k < KT - 1 else v_done, 1)
                    if k == 0:
                        pe.wait_ge(g_rows_ready, b + 1)
                        for j in range(NC):
                            last = pe.transpose(sco[:, chunk(j)], silu_zp[:, chunk(j)], ident)
                        last.then_inc(gates_T, 1)
                    if k == 2:
                        bro_wait(0)
                        pe.wait_ge(lf_ready, b + 1)
                        pe.matmul(bro[:, 0:16], tri, lf[:, :], start=True, stop=True)
                        pe.matmul(bro[:, 16:32], col(ones, 0), lf[:, :], start=True, stop=True).then_inc(bro_full, 1)
                    if k == 4:
                        bro_wait(1)
                        pe.wait_ge(a_ready, b + 1)
                        pe.transpose(bro[:, chunk(0)], a_pad[:, :], ident).then_inc(bro_full, 1)
                    if k == 6:
                        bro_wait(2)
                        pe.wait_ge(diag_ready, b + 1)
                        pe.matmul(bro[:, 0:16], col(ones, 0), diag[:, :], start=True, stop=True).then_inc(bro_full, 1)
                bro_wait(3)
                pe.wait_ge(m_ready, b + 1)
                pe.transpose(bro[:, chunk(0)], m_row[:, :], ident).then_inc(bro_full, 1)

                for name, i in TILES[:16]:
                    tile(name, i)

                def heads_to_scores(j):
                    if j == 0:
                        pe.wait_ge(qk_ready, b * 8 + 8)
                        pe.wait_ge(v_copied_dve, b + 1)
                        pe.wait_ge(v_copied_act, b + 1)
                        pe.wait_ge(inter_row_ready, b + 1)
                    reach(pe, sco_free, b * S_USES + SCO["qk", j])
                    for h in range(NH):
                        last = pe.matmul(sco[:, chunk(h)], kT[:, h, chunk(j)], qT[:, h, chunk(j)], start=True, stop=True)
                    last.then_inc(sco_full, 1)
                    bro_wait(4 + 2 * j)
                    for h in range(NH):
                        last = pe.matmul(bro[:, chunk(h)], col(cst, K_ID + NH * j + h), m_row[:, :], start=True, stop=True)
                    last.then_inc(bro_full, 1)

                def keys_transposed(j):
                    reach(pe, c_done, b * NC + j)
                    for h in range(NH):
                        last = pe.transpose(kv[1][:, chunk(h)], kT[:, h, chunk(j)], ident)
                    last.then_inc(k_T, 1)

                def inter_rows(j):
                    bro_wait(5 + 2 * j)
                    for h in range(NH):
                        last = pe.matmul(bro[:, chunk(h)], col(cst, K_ID + NH * j + h), inter_row[:, :],
                                         start=True, stop=True)
                    last.then_inc(bro_full, 1)

                def numerator_and_update(j):
                    pe.wait_ge(sco_free, b * S_USES + (SCO["qk", j] + 1))
                    pe.wait_ge(bro_free, b * B_USES + (6 + 2 * j))
                    reach(pe, h_ready, b * NC + j)
                    for h in range(NH):
                        dst = num[h // 2][:, 129 * (h % 2):129 * (h % 2) + 129]
                        pe.matmul(dst, dmat[:, h, :], v[:, j, h, :], start=True, stop=False)
                        last = pe.matmul(dst, q_in[:, h, :], cmem[:, h, :], start=False, stop=True)
                    last.then_inc(num_done, 1)
                    pe.wait_ge(k_w_ready, b * NC + (j + 1))
                    for h in range(NH):
                        last = pe.matmul(kv[h // 2][:, 129 * (h % 2):129 * (h % 2) + 129], k_w[:, h, :], v[:, j, h, :],
                                         start=True, stop=True)
                    last.then_inc(kv_done, 1)

                def pool_map(g):
                    dst = acc_wait("y", g)
                    pe.wait_ge(pooled_ready, b * NH + (g + 1))
                    pe.matmul(dst[:, :], wpool[:, g, :], acc_cv[:, HALO:], start=True, stop=True).then_inc(acc_full, 1)

                def hm_transposed(j):
                    pe.wait_ge(sco_free, b * S_USES + SCO["hm", j])
                    pe.wait_ge(hm_ready, b * NC + (j + 1))
                    for h in range(NH):
                        last = pe.transpose(sco[:, chunk(h)], hm[:, h, :], ident)
                    last.then_inc(sco_full, 1)

                for j in range(NC):
                    heads_to_scores(j)
                    tile("u", j)
                    keys_transposed(j)
                    if j > 0:
                        pool_map(j - 1)
                        hm_transposed(j - 1)
                    inter_rows(j)
                    tile("zp", j)
                    numerator_and_update(j)
                pool_map(3)

                def out_half(i):
                    j, cols = i // 2, slice(512 * (i % 2), 512 * (i % 2) + 512)
                    dst = acc_wait("out", i)
                    if i % 2 == 0:
                        pe.wait_ge(m_lo, b * NC + (j + 1))
                    for h in range(NH):
                        split3(dst[:, :], mixm_hi[:, j % 2, h, :], mixm_lo[:, j % 2, h, :],
                               wo_hi[:, NH + h, cols], wo_lo[:, NH + h, cols], h == 0, False)
                    if i == 0:
                        pe.wait_ge(y_lo, b * NH + NH)
                    for g in range(NH):
                        last = split3(dst[:, :], mixp_hi[:, g, chunk(j)], mixp_lo[:, g, chunk(j)],
                                      wo_hi[:, g, cols], wo_lo[:, g, cols], False, g == NH - 1)
                    last.then_inc(acc_full, 1)

                def prep_next(p):
                    if not last_block:
                        if p == 0:
                            pe.wait_ge(h_ready, b * NC + NC)
                        prep(b + 1, p)

                for i in range(8):
                    out_half(i)
                    if i == 1:
                        hm_transposed(3)
                    if i % 2 == 0:
                        prep_next(i)
                        prep_next(i + 1)

            one_block(0, False)
            with pe.Fori(1, NB - 1) as b:
                one_block(b, False)
            one_block(NB - 1, True)

        @block.scalar
        def _(act):
            def split_w(b, m):
                if b is None:
                    act.wait_ge(w_loaded[m % RING], 16)
                else:
                    act.wait_ge(w_loaded[m % RING], 16 * (b * WU + (m // RING + 1)))
                    used_wait(b, m - RING)
                act.activation(w_hi[:, m % RING, :], w_raw[:, m % RING, :], ACT.Copy).then_inc(w_hi_done, 1)

            def used_wait(b, m):
                if m < V_UNITS - 1:
                    act.wait_ge(w_used, b * 31 + (m + 1))
                elif m == V_UNITS - 1:
                    act.wait_ge(v_done, b + 1)
                else:
                    t, half = divmod(m - V_UNITS, 2)
                    if half == 0:
                        act.wait_ge(w_used, b * 31 + (V_UNITS - 1 + t + 1))
                    else:
                        act.wait_ge(acc_full, b * TASKS + (TASK[TILES[t]] + 1))

            def prep_sq(nb, c):
                act.wait_ge(x_loaded[c % 2], 16 * (nb * 2 + (c // 2 + 1)))
                act.activation(junk, x_in[:, c % 2, :], ACT.Square,
                               accum_out=x_sq[:, c % 2:c % 2 + 1]).then_inc(x_sq_done, 1)

            def prep_hi(nb, p):
                act.wait_ge(h_full, nb * PREPS + (p + 1))
                act.activation(hT_hi[:, 4 * (p % 2):4 * (p % 2) + 4, chunk(p // 2)], full[p % 2][:, :, :],
                               ACT.Copy).then_inc(h_hi, 1)

            act.wait_ge(par_ready, 1)
            act.activation(tanh[:, 0:KT], par[:, C_C:C_C + KT], ACT.Tanh, scale=0.5).then_inc(c_tanh, 1)
            act.wait_ge(silu_c_ready, 1)
            prep_sq(0, 0)
            act.wait_ge(x_sq_done, 1)
            prep_sq(0, 1)
            act.wait_ge(wg_loaded, 16)
            act.activation(wg_hi[:, :, :], wg_raw[:, :, :], ACT.Copy).then_inc(wg_hi_done, 1)
            for m in range(4):
                split_w(None, m)
            for p in range(PREPS):
                prep_hi(0, p)
                if p in (1, 3):
                    act.wait_ge(x_sq_done, 2 + p // 2)
                    prep_sq(0, 2 + p // 2)
            for k in range(KT):
                act.wait_ge(wout_scaled, k + 1)
                act.activation(wo_hi[:, k, :], x_res[:, k % 2, :], ACT.Copy).then_inc(wout_hi_done, 1)

            def one_block(b, last_block):
                def acc_wait(name, i):
                    t = TASK[name, i]
                    act.wait_ge(acc_full, b * TASKS + (t + 1))
                    return acc[t % 2], acc_free[t % 2]

                def tanh_wait(n):
                    if n == 0:
                        act.wait_ge(x_sq_done, b * NC + NC)
                        reach(act, o_sq_done, b * NC)
                        return
                    name, i = TANH_TILES[n - 1]
                    if name in "qk":
                        act.wait_ge(qk_ready, b * 8 + n)
                    else:
                        t = TASK[name, i]
                        act.wait_ge(acc_free[t % 2], b * (TASKS // 2) + (t // 2 + 1))

                act.wait_ge(g_abs_done, b + 1)
                act.activation(g_e[:, :], g_abs[:, :], ACT.Exp, scale=-1.0).then_inc(g_exp_done, 1)
                act.wait_ge(g_exp_done, b + 1)
                act.activation(g_e[:, :], g_e[:, :], ACT.Ln, bias=1.0).then_inc(g_ln_done, 1)
                for m in range(4, 10):
                    split_w(b, m)
                act.wait_ge(m_ready, b + 1)
                act.activation(inter_row[0:16, :], m_row[0:16, :], ACT.Exp, scale=-1.0,
                               bias=mp_col[:, :]).then_inc(inter_row_ready, 1)
                split_w(b, 10)
                act.wait_ge(v_done, b + 1)
                for j in range(2):
                    last = act.activation(v[:, j, :, 0:P], v_bank[j][:, :].rearrange("p (h d) -> p h d", d=P), ACT.Copy)
                last.then_inc(v_copied_act, 1)
                split_w(b, 11)
                act.wait_ge(expo_ready, b + 1)
                act.activation(expo[:, :, :], expo[:, :, :], ACT.Exp, scale=-1.0).then_inc(expo_done, 1)

                for t, (name, i) in enumerate(TILES[:16]):
                    m = V_UNITS + 2 * t + 4
                    split_w(b, m)
                    src, free = acc_wait(name, i)
                    if name in "qk":
                        if t > 1:
                            act.wait_ge(shifted_free, b * 8 + (t - 1))
                        else:
                            reach(act, pooled_ready, b * NH)
                        act.activation(shifted[:, t % 2, HALO:], src[:, :], ACT.Copy).then_inc(free, 1)
                        split_w(b, m + 1)
                        act.wait_ge(conv_done, b * 8 + (t + 1))
                        tanh_wait(t)
                        act.activation(tanh[:, :], acc_cv[:, HALO:], ACT.Tanh, scale=0.5).then_inc(tanh_ready, 1)
                    else:
                        tanh_wait(t)
                        if name == "z":
                            act.activation(tanh[:, :], src[:, :], ACT.Tanh, scale=0.5).then_inc(tanh_ready, 1)
                        else:
                            act.activation(tanh[:, :], src[:, :], ACT.Tanh, scale=0.5).then_inc(o_tanh, 1)
                            act.wait_ge(o_tanh, b * NH + (i + 1))
                            act.activation(tanh[:, :], tanh[:, :], ACT.Identity, scale=mg4[:, i:i + 1],
                                           bias=mg4[:, i:i + 1]).then_inc(tanh_ready, 1)
                        split_w(b, m + 1)

                def squares(j):
                    act.wait_ge(h_ready, b * NC + (j + 1))
                    for h in range(NH):
                        last = act.activation(junk[:, chunk(h)], hm[:, h, :], ACT.Square, accum_out=h_sq[:, h:h + 1])
                    last.then_inc(h_sq_done, 1)

                def y_high(g):
                    t = TASK["y", g]
                    act.wait_ge(acc_free[t % 2], b * (TASKS // 2) + (t // 2 + 1))
                    act.activation(mixp_hi[:, g, :], silu_zp[:, :], ACT.Copy).then_inc(y_hi, 1)

                def m_high(j):
                    act.wait_ge(sco_free, b * S_USES + (SCO["hm", j] + 1))
                    if j >= 2:
                        act.wait_ge(acc_full, b * TASKS + (TASK["out", 2 * j - 3] + 1))
                    act.activation(mixm_hi[:, j % 2, :, :], oz[:, :, chunk(j)], ACT.Copy).then_inc(m_hi, 1)

                for j in range(NC):
                    m = unit0("u", j) + 4
                    if j > 0:
                        squares(j - 1)
                    act.wait_ge(bro_free, b * B_USES + (5 + 2 * j))
                    act.activation(dmat[:, :, :], dmat[:, :, :], ACT.Exp, scale=-1.0).then_inc(d_exp, 1)
                    if not last_block or m < UNITS:
                        split_w(b, m)
                    src, free = acc_wait("u", j)
                    if j > 0:
                        act.wait_ge(pooled_ready, b * NH + j)
                    else:
                        act.wait_ge(shifted_free, b * 8 + 8)
                    act.activation(shifted[:, 0, HALO:], src[:, :], ACT.Copy).then_inc(free, 1)
                    if not last_block or m < UNITS:
                        split_w(b, m + 1)
                    if j > 0:
                        y_high(j - 1)
                    if j >= 2:
                        m_high(j - 2)
                    if not last_block or m + 2 < UNITS:
                        split_w(b, m + 2)
                    reach(act, h_sq_done, b * NC + j)
                    if j >= 2 and not last_block:
                        prep_sq(b + 1, j - 2)
                        act.wait_ge(x_sq_done, (b + 1) * NC + (j - 1))
                    src, free = acc_wait("zp", j)
                    tanh_wait(16 + j)
                    act.activation(tanh[:, :], src[:, :], ACT.Tanh, scale=0.5).then_inc(tanh_ready, 1)
                    if not last_block or m + 2 < UNITS:
                        split_w(b, m + 3)

                def out_sq(j):
                    t = TASK["out", 2 * j + 1]
                    act.wait_ge(acc_free[t % 2], b * (TASKS // 2) + (t // 2 + 1))
                    if j == 0:
                        act.wait_ge(h_sq_done, b * NC + NC)
                    elif j < 3 and not last_block:
                        act.wait_ge(x_sq_done, (b + 1) * NC + (j + 2))
                    else:
                        act.wait_ge(o_sq_done, b * NC + j)
                    act.activation(junk, x_res[:, j % 2, :], ACT.Square,
                                   accum_out=o_sq[:, j % 2:j % 2 + 1]).then_inc(o_sq_done, 1)

                squares(3)
                y_high(3)
                for i in range(8):
                    if i % 2 == 0 and not last_block:
                        prep_hi(b + 1, i)
                        prep_hi(b + 1, i + 1)
                    if i % 2:
                        out_sq(i // 2)
                    if i in (1, 3) and not last_block:
                        act.wait_ge(o_sq_done, b * NC + (i // 2 + 1))
                        prep_sq(b + 1, 2 + i // 2)
                    if i in (1, 3):
                        m_high(2 + i // 2)

            one_block(0, False)
            with act.Fori(1, NB - 1) as b:
                one_block(b, False)
            one_block(NB - 1, True)

        @block.gpsimd
        def _(pool):
            def low_w(b, m):
                pool.wait_ge(w_hi_done, m + 1 if b is None else b * UNITS + (m + 1))
                nc.gpsimd.tensor_tensor(w_lo[:, m % RING, :], w_raw[:, m % RING, :], w_hi[:, m % RING, :].bitcast(F32),
                                        ALU.subtract).then_inc(w_lo_done, 1)

            def prep_lo(nb, p):
                pool.wait_ge(h_hi, nb * PREPS + (p + 1))
                dst = slice(4 * (p % 2), 4 * (p % 2) + 4), chunk(p // 2)
                nc.gpsimd.tensor_tensor(hT_lo[:, dst[0], dst[1]], full[p % 2][:, :, :], hT_hi[:, dst[0], dst[1]].bitcast(F32),
                                        ALU.subtract).then_inc(h_lo, 1)

            def rsqrt(var_done, value, dst, src, done):
                n = src.shape[1]
                pool.wait_ge(var_done, value)
                nc.gpsimd.tensor_tensor(dst, src, mhalf[:, 0:n], ALU.pow).then_inc(done, 1)

            def x_rsqrt(nb, c):
                rsqrt(x_var_done, nb * NC + (c + 1), x_rs[:, c % 2:c % 2 + 1], x_var[:, c % 2:c % 2 + 1], x_rs_done)

            nc.gpsimd.memset(mhalf[:, :], -0.5).then_inc(mhalf_ready, 1)
            pool.wait_ge(mhalf_ready, 1)
            x_rsqrt(0, 0)
            x_rsqrt(0, 1)
            pool.wait_ge(wg_hi_done, 1)
            nc.gpsimd.tensor_tensor(wg_lo[:, :, :], wg_raw[:, :, :], wg_hi[:, :, :].bitcast(F32),
                                    ALU.subtract).then_inc(wg_lo_done, 1)
            for m in range(4):
                low_w(None, m)
            for p in range(PREPS):
                prep_lo(0, p)
                if p in (1, 3):
                    x_rsqrt(0, 2 + p // 2)

            def one_block(b, last_block):
                def h_rsqrt(j):
                    rsqrt(h_var_done, b * NC + (j + 1), h_rs[:, :], h_var[:, :], h_rs_done)

                for m in range(4, 40):
                    low_w(b, m)
                for m0 in range(44, 60, 4):
                    j = (m0 - 44) // 4
                    if j == 0:
                        for m in range(40, 44):
                            low_w(b, m)
                    if j > 0:
                        h_rsqrt(j - 1)
                    for m in range(m0, m0 + 4):
                        if m < UNITS or not last_block:
                            low_w(b, m)
                        if m == m0 + 2 and j >= 2 and not last_block:
                            x_rsqrt(b + 1, j - 2)
                h_rsqrt(3)
                for i in range(8):
                    if i % 2 == 0 and not last_block:
                        prep_lo(b + 1, i)
                        prep_lo(b + 1, i + 1)
                    if i in (1, 3) and not last_block:
                        x_rsqrt(b + 1, 2 + i // 2)
                    if i % 2:
                        j = i // 2
                        rsqrt(o_var_done, b * NC + (j + 1), o_rs[:, j % 2:j % 2 + 1], o_var[:, j % 2:j % 2 + 1], o_rs_done)

            one_block(0, False)
            with pool.Fori(1, NB - 1) as b:
                one_block(b, False)
            one_block(NB - 1, True)

        @block.vector
        def _(dve):
            V = nc.vector
            count = [0]
            base = [0]
            latest = [None]

            def step(ins):
                ins.then_inc(dve_step, 1)
                count[0] += 1
                did(dve_step, base[0] + count[0])

            def did(sem, value):
                latest[0] = (sem, value)

            def in_turn():
                reach(dve, *latest[0])

            def prep_scale(nb, c):
                s = slice(c % 2, c % 2 + 1)
                in_turn()
                dve.wait_ge(x_rs_done, nb * NC + (c + 1))
                V.tensor_scalar(x_in[:, c % 2, :], x_in[:, c % 2, :], x_rs[:, s], None, ALU.mult).then_inc(x_scaled, 1)
                did(x_scaled, nb * NC + (c + 1))

            def prep_var(nb, c):
                s = slice(c % 2, c % 2 + 1)
                in_turn()
                dve.wait_ge(x_sq_done, nb * NC + (c + 1))
                V.tensor_scalar(x_var[:, s], x_sq[:, s], 1.0 / D, EPS, ALU.mult, ALU.add).then_inc(x_var_done, 1)
                did(x_var_done, nb * NC + (c + 1))

            def prep_full(nb, p, first=False):
                in_turn()
                dve.wait_ge(x_T, nb * PREPS + (p + 1))
                if not first:
                    dve.wait_ge(h_lo, nb * PREPS + (p - 1))
                for i in range(4):
                    k = 4 * (p % 2) + i
                    last = V.tensor_scalar(full[p % 2][:, i, :], num[p % 2][:, chunk(i)], gain[:, k:k + 1], shift[:, k:k + 1],
                                           ALU.mult, ALU.add)
                last.then_inc(h_full, 1)
                did(h_full, nb * PREPS + (p + 1))

            V.memset(x_res[:, 0, 0:P], 0.0).then_inc(rows_zeroed, 1)
            for t in (halo_qk[:, :, :], halo_u[:, :, :], cmem[:, :, :], a_pad[:, :], m_row[:, :], inter_row[:, :],
                      diag[:, :], m_prev[:, :], silu_zp[:, :]):
                V.memset(t, 0.0)
            V.memset(ones[:, :], 1.0)
            for t in range(2):
                V.memset(shifted[:, t, :], 0.0)
            step(V.memset(v[:, :, :, P:P + 1], 1.0))
            dve.wait_ge(par_T, 1)
            V.tensor_copy(par[:, :], kv[0][:, 0:C_END]).then_inc(par_ready, 1)
            did(par_ready, 1)
            dve.wait_ge(par_ready, 1)
            dve.wait_ge(c_tanh, 1)
            step(V.scalar_tensor_tensor(silu_c[:, :], tanh[:, 0:KT], 1.0, par[:, C_C:C_C + KT], ALU.add, ALU.mult))
            in_turn()
            V.tensor_scalar(silu_c[:, :], silu_c[:, :], 0.5, None, ALU.mult).then_inc(silu_c_ready, 1)
            did(silu_c_ready, 1)
            V.tensor_scalar(mg4[:, :], par[:, C_MG:C_MG + NH], 0.25, None, ALU.mult)
            V.tensor_scalar(ls2[:, :], par[:, C_LS:C_LS + NH], 0.5, None, ALU.mult)
            for c0 in range(2):
                prep_var(0, c0)
                prep_scale(0, c0)
            dve.wait_ge(ada_used, 8)
            step(V.tensor_tensor(shift[:, :], kv[1][:, 0:KT], par[:, C_BA:C_BA + KT], ALU.add))
            step(V.tensor_tensor(gain[:, :], kv[1][:, KT:2 * KT], par[:, C_BA + KT:C_BA + 2 * KT], ALU.add))
            in_turn()
            step(V.scalar_tensor_tensor(gain[:, :], gain[:, :], 1.0, par[:, C_NG:C_NG + KT], ALU.add, ALU.mult))
            in_turn()
            for p in range(PREPS):
                prep_full(0, p, p < 2)
                if p in (1, 3):
                    c_next = 2 + p // 2
                    prep_var(0, c_next)
                    prep_scale(0, c_next)
            dve.wait_ge(ada_used, 12)
            V.tensor_tensor(gate_col[:, :], sco[:, 16:16 + KT], par[:, C_BA + 2 * KT:C_BA + 3 * KT],
                            ALU.add).then_inc(gate_ready, 1)
            dve.wait_ge(gate_bc, 1)
            did(gate_ready, 1)
            for k in range(KT):
                in_turn()
                dve.wait_ge(wout_loaded[k % 2], 16 * (k // 2 + 1))
                for n in range(2):
                    s = slice(512 * n, 512 * n + 512)
                    last = V.tensor_tensor(x_res[:, k % 2, s], x_res[:, k % 2, s], kv[n][:, :], ALU.mult)
                last.then_inc(wout_scaled, 1)
                dve.wait_ge(wout_scaled, k + 1)
                dve.wait_ge(wout_hi_done, k + 1)
                V.tensor_tensor(wo_lo[:, k, :], x_res[:, k % 2, :], wo_hi[:, k, :].bitcast(F32),
                                ALU.subtract).then_inc(wout_lo_done, 1)
                did(wout_lo_done, k + 1)
            in_turn()
            dve.wait_ge(misc_loaded, 48)
            dve.wait_ge(fg_loaded, 16)
            dve.wait_ge(wg_lo_done, 1)
            step(V.memset(den[:, :], 0.0))
            in_turn()
            V.memset(rden[:, :], 0.0).then_inc(setup_done, 1)
            dve.wait_ge(setup_done, 1)
            setup_steps = count[0]

            def one_block(b, last_block):
                count[0] = 0
                base[0] = b * DVE_STEPS + setup_steps

                def bro_read(u):
                    dve.wait_ge(bro_full, b * B_USES + (u + 1))

                def acc_wait(name, i):
                    t = TASK[name, i]
                    dve.wait_ge(acc_full, b * TASKS + (t + 1))
                    return acc[t % 2], acc_free[t % 2]

                did(o_ready, b * NC)
                in_turn()
                dve.wait_ge(gates_done, b + 1)
                V.tensor_copy(silu_zp[0:8, :], sco[0:8, :]).then_inc(g_rows_ready, 1)
                dve.wait_ge(gates_T, b + 1)
                V.tensor_tensor(g_pre[:, :, :], sco[:, :].rearrange("p (c g) -> p c g", g=P)[:, :, 0:8],
                                bg[:, :].unsqueeze(1).broadcast_to([P, NC, 8]), ALU.add).then_inc(sco_free, 1)
                dve.wait_ge(sco_free, b * S_USES + 1)
                g_i, g_f = g_pre[:, :, 0:NH], g_pre[:, :, NH:2 * NH]
                lf_v = lf[:, :].rearrange("p (c h) -> p c h", h=NH)
                V.scalar_tensor_tensor(g_abs[:, :].rearrange("p (c h) -> p c h", h=NH), g_f, -1.0, g_f, ALU.mult,
                                       ALU.max).then_inc(g_abs_done, 1)
                did(g_abs_done, b + 1)
                in_turn()
                dve.wait_ge(g_ln_done, b + 1)
                V.scalar_tensor_tensor(lf_v, g_f, 0.0, g_e[:, :].rearrange("p (c h) -> p c h", h=NH), ALU.min,
                                       ALU.subtract).then_inc(lf_ready, 1)
                did(lf_ready, b + 1)
                in_turn()
                bro_read(0)
                V.tensor_copy(b_cum[:, :], bro[:, 0:32]).then_inc(bro_free, 1)
                dve.wait_ge(bro_free, b * B_USES + 1)
                V.tensor_tensor(a_pad[:, 0:16].rearrange("p (c h) -> p c h", h=NH), g_i,
                                b_cum[:, 0:16].rearrange("p (c h) -> p c h", h=NH), ALU.subtract).then_inc(a_ready, 1)
                did(a_ready, b + 1)
                in_turn()
                bro_read(1)
                V.tensor_copy(aT, bro[0:16, chunk(0)]).then_inc(bro_free, 1)
                dve.wait_ge(bro_free, b * B_USES + 2)
                step(V.tensor_tensor_scan(cmax, aT, aT, -3.0e38, ALU.max, ALU.max))
                in_turn()
                V.tensor_scalar(diag[0:16, :], ident[0:16, 0:16], cmax[:, P - 1:P], None, ALU.mult).then_inc(diag_ready, 1)
                did(diag_ready, b + 1)
                in_turn()
                bro_read(2)
                for j in range(NC):
                    s, n = slice(NH * j, NH * j + NH), slice(NH * j + NH, NH * j + 2 * NH)
                    step(V.tensor_tensor(m_last[:, s], m_prev[:, s], bro[:, s], ALU.max))
                    in_turn()
                    ins = V.tensor_tensor(m_prev[:, n], m_last[:, s], b_cum[:, 16 + NH * j:16 + NH * j + NH], ALU.add)
                    if j < NC - 1:
                        step(ins)
                    else:
                        ins.then_inc(bro_free, 1)
                        did(bro_free, b * B_USES + 3)
                    in_turn()
                step(V.tensor_tensor(mp_diag, m_prev[0:16, 0:16], ident[0:16, 0:16], ALU.mult))
                in_turn()
                step(V.tensor_reduce(mp_col[:, :], mp_diag, AX.X, ALU.add))
                in_turn()
                V.tensor_scalar(m_row[0:16, :], cmax, mp_col[:, :], None, ALU.max).then_inc(m_ready, 1)
                did(m_ready, b + 1)
                step(V.tensor_tensor(expo[:, 1, :], m_last[:, :], a_pad[:, 0:16], ALU.subtract))
                step(V.tensor_tensor(expo[:, 2, :], m_last[:, :], m_prev[:, 0:16], ALU.subtract))
                bro_read(3)
                V.tensor_tensor(expo[:, 0, :], b_cum[:, 0:16], bro[:, 0:16], ALU.add).then_inc(bro_free, 1)
                dve.wait_ge(bro_free, b * B_USES + 4)
                V.tensor_copy(m_prev[:, 0:NH], m_prev[:, 16:20]).then_inc(expo_ready, 1)
                did(expo_ready, b + 1)
                in_turn()
                dve.wait_ge(v_done, b + 1)
                for j in range(2, 4):
                    last = V.tensor_copy(v[:, j, :, 0:P], v_bank[j][:, :].rearrange("p (h d) -> p h d", d=P))
                last.then_inc(v_copied_dve, 1)
                did(v_copied_dve, b + 1)

                for t, (name, i) in enumerate(TILES[:16]):
                    in_turn()
                    if name in "qk":
                        sh = shifted[:, t % 2, :]
                        tap = [par[:, C_CW + 8 * n + t:C_CW + 8 * n + t + 1] for n in range(CW)]
                        step(V.tensor_copy(sh[:, HALO - 3:HALO], halo_qk[:, t, :]))
                        dve.wait_ge(acc_free[t % 2], b * (TASKS // 2) + (t // 2 + 1))
                        step(V.tensor_scalar(acc_cv[:, HALO:], sh[:, HALO:], tap[3], par[:, C_CB + t:C_CB + t + 1],
                                             ALU.mult, ALU.add))
                        for n in (2, 1, 0):
                            in_turn()
                            ins = V.scalar_tensor_tensor(acc_cv[:, HALO:], sh[:, HALO - 3 + n:HALO - 3 + n + BLK], tap[n],
                                                         acc_cv[:, HALO:], ALU.mult, ALU.add)
                            if n:
                                step(ins)
                            else:
                                ins.then_inc(conv_done, 1)
                                did(conv_done, b * 8 + (t + 1))
                        V.tensor_copy(halo_qk[:, t, :], sh[:, HALO + BLK - 3:HALO + BLK]).then_inc(shifted_free, 1)
                        dve.wait_ge(tanh_ready, b * TANHS + (t + 1))
                        dve.wait_ge(conv_done, b * 8 + (t + 1))
                        V.scalar_tensor_tensor((qT if name == "q" else kT)[:, i, :], tanh[:, :], 1.0, acc_cv[:, HALO:],
                                               ALU.add, ALU.mult).then_inc(qk_ready, 1)
                        did(qk_ready, b * 8 + (t + 1))
                    elif name == "z":
                        src, free = acc_wait(name, i)
                        dve.wait_ge(tanh_ready, b * TANHS + (t + 1))
                        V.scalar_tensor_tensor(oz[:, i, :], tanh[:, :], 1.0, src[:, :], ALU.add, ALU.mult).then_inc(free, 1)
                        did(free, b * (TASKS // 2) + (TASK[name, i] // 2 + 1))
                    else:
                        src, free = acc_wait(name, i)
                        dve.wait_ge(tanh_ready, b * TANHS + (t + 1))
                        V.tensor_tensor(oz[:, i, :], tanh[:, :], oz[:, i, :], ALU.mult).then_inc(free, 1)
                        did(free, b * (TASKS // 2) + (TASK[name, i] // 2 + 1))

                def rows(t):
                    return t.unsqueeze(2).broadcast_to([P, t.shape[1], P])

                def heads(j):
                    in_turn()
                    dve.wait_ge(num_done, b * NC + (j + 1))
                    pairs = [t[:, 0:258].rearrange("p (h d) -> p h d", d=P + 1) for t in num]
                    for q in range(2):
                        n = slice(NH * j + 2 * q, NH * j + 2 * q + 2)
                        step(V.scalar_tensor_tensor(den[:, 2 * q:2 * q + 2].unsqueeze(2), pairs[q][:, :, P:P + 1], -1.0,
                                                    expo[:, 0, n].unsqueeze(2), ALU.mult, ALU.max))
                    in_turn()
                    for q in range(2):
                        step(V.tensor_tensor(den[:, 2 * q:2 * q + 2].unsqueeze(2), den[:, 2 * q:2 * q + 2].unsqueeze(2),
                                             pairs[q][:, :, P:P + 1], ALU.max))
                    in_turn()
                    step(V.reciprocal(rden[:, :], den[:, :]))
                    in_turn()
                    for q in range(2):
                        last = V.tensor_tensor(hm[:, 2 * q:2 * q + 2, :], pairs[q][:, :, 0:P], rows(rden[:, 2 * q:2 * q + 2]),
                                               ALU.mult)
                    last.then_inc(h_ready, 1)
                    did(h_ready, b * NC + (j + 1))

                def update_c(j):
                    in_turn()
                    dve.wait_ge(kv_done, b * NC + (j + 1))
                    for h in range(NH):
                        last = V.scalar_tensor_tensor(cmem[:, h, :], cmem[:, h, :], expo[:, 2, NH * j + h:NH * j + h + 1],
                                                      kv[h // 2][:, 129 * (h % 2):129 * (h % 2) + 129], ALU.mult, ALU.add)
                    last.then_inc(c_done, 1)
                    did(c_done, b * NC + (j + 1))

                def head_var(j):
                    in_turn()
                    dve.wait_ge(h_sq_done, b * NC + (j + 1))
                    V.tensor_scalar(h_var[:, :], h_sq[:, :], 1.0 / P, EPS, ALU.mult, ALU.add).then_inc(h_var_done, 1)
                    did(h_var_done, b * NC + (j + 1))

                def head_norm(j):
                    dve.wait_ge(h_rs_done, b * NC + (j + 1))
                    in_turn()
                    V.tensor_tensor(hm[:, :, :], hm[:, :, :], rows(h_rs[:, :]), ALU.mult).then_inc(hm_ready, 1)
                    did(hm_ready, b * NC + (j + 1))

                def y_mixed(g):
                    in_turn()
                    src, free = acc_wait("y", g)
                    V.scalar_tensor_tensor(silu_zp[:, :], src[:, :], ls2[:, g:g + 1], silu_zp[:, :], ALU.mult,
                                           ALU.mult).then_inc(free, 1)
                    did(free, b * (TASKS // 2) + (TASK["y", g] // 2 + 1))

                def y_low(g):
                    in_turn()
                    dve.wait_ge(y_hi, b * NH + (g + 1))
                    V.tensor_tensor(mixp_lo[:, g, :], silu_zp[:, :], mixp_hi[:, g, :].bitcast(F32),
                                    ALU.subtract).then_inc(y_lo, 1)
                    did(y_lo, b * NH + (g + 1))

                def m_mixed(j):
                    in_turn()
                    dve.wait_ge(sco_full, b * SCO_FULLS + SCO["hm", j])
                    V.tensor_tensor(oz[:, :, chunk(j)], sco[:, :].rearrange("p (h t) -> p h t", t=P), oz[:, :, chunk(j)],
                                    ALU.mult).then_inc(sco_free, 1)
                    did(sco_free, b * S_USES + (SCO["hm", j] + 1))

                def m_low(j):
                    in_turn()
                    dve.wait_ge(m_hi, b * NC + (j + 1))
                    V.tensor_tensor(mixm_lo[:, j % 2, :, :], oz[:, :, chunk(j)], mixm_hi[:, j % 2, :, :].bitcast(F32),
                                    ALU.subtract).then_inc(m_lo, 1)
                    did(m_lo, b * NC + (j + 1))

                def windows(g):
                    sh, levels = shifted[:, 0, :], g + 1
                    in_turn()
                    step(V.tensor_copy(sh[:, 0:HALO], halo_u[:, g, :]))
                    t = TASK["u", g]
                    dve.wait_ge(acc_free[t % 2], b * (TASKS // 2) + (t // 2 + 1))
                    src = sh
                    for n in range(levels):
                        dst, lo, by = (shifted[:, 1, :], acc_cv[:, :])[n % 2], 2 ** (n + 1) - 1, 2 ** n
                        in_turn()
                        step(V.tensor_tensor(dst[:, lo:], src[:, lo:], src[:, lo - by:HALO + BLK - by], ALU.add))
                        src = dst
                    in_turn()
                    step(V.tensor_tensor(src[:, HALO:HALO + 15], src[:, HALO:HALO + 15], warm[:, g, :], ALU.mult))
                    step(V.tensor_copy(halo_u[:, g, :], sh[:, BLK:]))
                    in_turn()
                    V.scalar_tensor_tensor(acc_cv[:, HALO:], src[:, HALO:], 1.0 / WINDOWS[g], sh[:, HALO:], ALU.mult,
                                           ALU.subtract).then_inc(pooled_ready, 1)
                    did(pooled_ready, b * NH + (g + 1))

                dve.wait_ge(expo_done, b + 1)
                for j in range(NC):
                    if j > 0:
                        heads(j - 1)
                        update_c(j - 1)
                    in_turn()
                    bro_read(4 + 2 * j)
                    for h in range(NH):
                        last = V.scalar_tensor_tensor(dmat[:, h, :], bro[:, chunk(h)], a_pad[:, NH * j + h:NH * j + h + 1],
                                                      bigm, ALU.subtract, ALU.add)
                    last.then_inc(bro_free, 1)
                    did(bro_free, b * B_USES + (5 + 2 * j))
                    in_turn()
                    dve.wait_ge(sco_full, b * SCO_FULLS + SCO["qk", j])
                    dve.wait_ge(d_exp, b * NC + (j + 1))
                    V.scalar_tensor_tensor(dmat[:, :, :].rearrange("p h t -> p (h t)"), sco[:, :], QK_SCALE,
                                           dmat[:, :, :].rearrange("p h t -> p (h t)"), ALU.mult,
                                           ALU.mult).then_inc(sco_free, 1)
                    did(sco_free, b * S_USES + (SCO["qk", j] + 1))
                    if j > 0:
                        head_var(j - 1)
                        head_norm(j - 1)
                        y_mixed(j - 1)
                        m_mixed(j - 1)
                    in_turn()
                    bro_read(5 + 2 * j)
                    V.scalar_tensor_tensor(q_in[:, :, :], qT[:, :, chunk(j)], QK_SCALE,
                                           bro[:, :].rearrange("p (h t) -> p h t", t=P), ALU.mult,
                                           ALU.mult).then_inc(bro_free, 1)
                    did(bro_free, b * B_USES + (6 + 2 * j))
                    dve.wait_ge(k_T, b * NC + (j + 1))
                    V.tensor_tensor(k_w[:, :, :], kv[1][:, :].rearrange("p (h d) -> p h d", d=P),
                                    rows(expo[:, 1, NH * j:NH * j + NH]), ALU.mult).then_inc(k_w_ready, 1)
                    did(k_w_ready, b * NC + (j + 1))
                    windows(j)
                    if j > 0:
                        y_low(j - 1)
                    if j >= 2:
                        m_low(j - 2)
                    if j >= 2 and not last_block:
                        prep_var(b + 1, j - 2)
                    in_turn()
                    src, free = acc_wait("zp", j)
                    dve.wait_ge(tanh_ready, b * TANHS + (17 + j))
                    V.scalar_tensor_tensor(silu_zp[:, :], tanh[:, :], 1.0, src[:, :], ALU.add, ALU.mult).then_inc(free, 1)
                    did(free, b * (TASKS // 2) + (TASK["zp", j] // 2 + 1))
                    if j >= 2 and not last_block:
                        prep_scale(b + 1, j - 2)

                def add_residual(i):
                    j, s = i // 2, slice(512 * (i % 2), 512 * (i % 2) + 512)
                    in_turn()
                    src, free = acc_wait("out", i)
                    if i % 2 == 0:
                        dve.wait_ge(res_loaded[j % 2], 16 * (b * 2 + (j // 2 + 1)))
                    V.tensor_tensor(x_res[:, j % 2, s], src[:, :], x_res[:, j % 2, s], ALU.add).then_inc(free, 1)
                    did(free, b * (TASKS // 2) + (TASK["out", i] // 2 + 1))

                def out_var(j):
                    s = slice(j % 2, j % 2 + 1)
                    in_turn()
                    dve.wait_ge(o_sq_done, b * NC + (j + 1))
                    V.tensor_scalar(o_var[:, s], o_sq[:, s], 1.0 / D, EPS, ALU.mult, ALU.add).then_inc(o_var_done, 1)
                    did(o_var_done, b * NC + (j + 1))

                def out_norm(j):
                    in_turn()
                    dve.wait_ge(o_rs_done, b * NC + (j + 1))
                    V.scalar_tensor_tensor(x_res[:, j % 2, :], x_res[:, j % 2, :], o_rs[:, j % 2:j % 2 + 1], fg[:, :],
                                           ALU.mult, ALU.mult).then_inc(o_ready, 1)
                    did(o_ready, b * NC + (j + 1))

                in_turn()
                step(V.memset(warm[:, :, :], 1.0))
                heads(3)
                update_c(3)
                y_mixed(3)
                head_var(3)
                y_low(3)
                head_norm(3)
                for i in range(8):
                    add_residual(i)
                    if i % 2 == 0 and not last_block:
                        prep_full(b + 1, i)
                        prep_full(b + 1, i + 1)
                    if i in (2, 4, 6):
                        out_norm(i // 2 - 1)
                    if i in (1, 3) and not last_block:
                        prep_var(b + 1, 2 + i // 2)
                    if i % 2:
                        out_var(i // 2)
                    if i == 1:
                        m_mixed(3)
                    if i in (1, 3):
                        m_low(2 + i // 2)
                    if i in (1, 3) and not last_block:
                        prep_scale(b + 1, 2 + i // 2)
                out_norm(3)
                assert count[0] == DVE_STEPS, count[0]

            one_block(0, False)
            with dve.Fori(1, NB - 1) as b:
                one_block(b, False)
            one_block(NB - 1, True)


INPUTS = ("x", "c", "norm_g", "w_ada", "b_ada", "w_in", "b_gates", "conv_w", "conv_b", "w_pool", "ls_pool",
          "mh_norm_g", "w_out", "final_g")


def constants():
    s, t = np.arange(P)[:, None], np.arange(P)[None, :]
    cor = [w / np.minimum(np.arange(1, 16), w) for w in WINDOWS]
    parts = [np.eye(P), s <= t, np.where(s > t, BIG, 0.0), np.tile(np.concatenate(cor), (P, 1))]
    return np.concatenate([np.asarray(a, np.float32) for a in parts], axis=1)


def kernel(**inputs):
    import concourse.bacc as bacc
    from concourse.bass_utils import run_bass_kernel_spmd

    nc = bacc.Bacc("TRN2", target_bir_lowering=False, num_devices=1, dynamic_dma_scratch_size=64)
    arrays = {name: np.ascontiguousarray(inputs[name]) for name in INPUTS}
    arrays["consts"] = constants()
    args = [nc.dram_tensor(n, a.shape, mybir.dt.from_np(a.dtype), kind="ExternalInput").ap() for n, a in arrays.items()]
    out = nc.dram_tensor("out", arrays["x"].shape, F32, kind="ExternalOutput").ap()
    build(nc, *args, out)
    r = run_bass_kernel_spmd(nc, [arrays], core_ids=[0])
    return r.results[0]["out"]
```

```python
from contextlib import ExitStack

import numpy as np

import concourse.bass as bass
from concourse import mybir

F32 = mybir.dt.float32
F32R = mybir.dt.float32r
BF16 = mybir.dt.bfloat16
ALU = mybir.AluOpType
ACT = mybir.ActivationFunctionType
AX = mybir.AxisListType

P = 128
D = 1024
KT = D // P
SEQ = 4096
BLK = 512
NB = SEQ // BLK
NC = BLK // P
NH = 4
CW = 4
WINDOWS = (2, 4, 8, 16)
EPS = 1e-6
OFF_U, OFF_ZP, OFF_Q, OFF_K, OFF_V, OFF_O, OFF_ZM, OFF_G = (512 * i for i in range(8))
QK_SCALE = 1.0 / (4.0 * float(np.sqrt(float(P))))
BIG = 1e38
HALO = 16

RING = 4
V_UNITS = KT
UNITS = V_UNITS + 2 * 24
WU = UNITS // RING
TASKS = 36
TANHS = 20
SCO_FULLS = 8
S_USES = 1 + SCO_FULLS
B_USES = 12
PREPS = 8
WOUT_TILE = 6
LO_ROW = 32
DVE_STEPS = 87
C_NG, C_C, C_BA, C_CW, C_CB, C_LS, C_MG, C_END = 0, 8, 16, 40, 72, 80, 84, 88
K_ID, K_TRI, K_BIG, K_END = 0, 128, 256, 384
K_COR = 15 * NH

TASK = {}
for _i in range(4):
    TASK["q", _i], TASK["k", _i], TASK["z", _i], TASK["o", _i] = _i, 4 + _i, 8 + _i, 12 + _i
TASK["u", 0], TASK["zp", 0] = 16, 17
for _i in range(1, 4):
    TASK["u", _i], TASK["y", _i - 1], TASK["zp", _i] = 15 + 3 * _i, 16 + 3 * _i, 17 + 3 * _i
TASK["y", 3] = 27
for _i in range(8):
    TASK["out", _i] = 28 + _i
SCO = {("qk", 0): 1, ("qk", 1): 2, ("hm", 0): 3, ("qk", 2): 4, ("hm", 1): 5, ("qk", 3): 6, ("hm", 2): 7, ("hm", 3): 8}
TILES = [(n, i) for n in ("q", "k", "z", "o") for i in range(4)] + [(n, i) for i in range(4) for n in ("u", "zp")]
TANH_TILES = TILES[:16] + [("zp", i) for i in range(4)]
OFFSET = {"q": OFF_Q, "k": OFF_K, "z": OFF_ZM, "o": OFF_O, "u": OFF_U, "zp": OFF_ZP}


def unit0(name, i):
    return V_UNITS + 2 * TILES.index((name, i))


def build(nc, x, c, norm_g, w_ada, b_ada, w_in, b_gates, conv_w, conv_b, w_pool, ls_pool, mh_norm_g,
          w_out, final_g, consts, out):
    with ExitStack() as ctx:
        def sb(name, shape, dt=F32):
            return ctx.enter_context(nc.sbuf_tensor("sb_" + name, shape, dt))

        def bank(name):
            return ctx.enter_context(nc.psum_tensor("ps_" + name, [P, 512], F32))

        def sem(name):
            return ctx.enter_context(nc.semaphore(name))

        hT_hi, hT_lo = sb("hT_hi", [P, KT, BLK], F32R), sb("hT_lo", [P, KT, BLK], F32R)
        wo_hi, wo_lo = sb("wo_hi", [P, KT, D], F32R), sb("wo_lo", [P, KT, D], F32R)
        w_raw = sb("w_raw", [P, RING, 512])
        w_hi, w_lo = sb("w_hi", [P, RING, 512], F32R), sb("w_lo", [P, RING, 512], F32R)
        wg_raw = sb("wg_raw", [P, KT, 8])
        wg_hi, wg_lo = sb("wg_hi", [P, KT, 8], F32R), sb("wg_lo", [P, KT, 8], F32R)
        qT, kT, oz = sb("qT", [P, NH, BLK]), sb("kT", [P, NH, BLK]), sb("oz", [P, NH, BLK])
        v = sb("v", [P, NC, NH, P + 1])
        mixp_hi, mixp_lo = sb("mixp_hi", [P, NH, BLK], F32R), sb("mixp_lo", [P, NH, BLK], F32R)
        mixm_hi, mixm_lo = sb("mixm_hi", [P, 2, NH, P], F32R), sb("mixm_lo", [P, 2, NH, P], F32R)
        shifted = sb("shifted", [P, 2, HALO + BLK])
        acc_cv = sb("acc_cv", [P, HALO + BLK])
        tanh = sb("tanh", [P, BLK])
        halo_qk, halo_u = sb("halo_qk", [P, 8, CW - 1]), sb("halo_u", [P, NH, HALO])
        silu_zp = sb("silu_zp", [P, BLK])
        dmat = sb("dmat", [P, NH, P])
        q_in = sb("q_in", [P, NH, P])
        k_w = sb("k_w", [P, NH, P])
        hm = q_in
        cmem = sb("cmem", [P, NH, P + 1])
        x_in = sb("x_in", [P, 2, D])
        x_res = sb("x_res", [P, 2, D])
        full = [dmat, k_w]
        junk = tanh[:, :].bitcast(BF16)
        fg = sb("fg", [P, D])
        wpool = sb("wpool", [P, NH, P])
        cst = sb("cst", [P, K_END])
        warm = sb("warm", [P, NH, 15])
        par = sb("par", [P, C_END])
        gain, shift = sb("gain", [P, KT]), sb("shift", [P, KT])
        silu_c = sb("silu_c", [P, KT])
        mg4, ls2 = sb("mg4", [P, NH]), sb("ls2", [P, NH])
        bg = sb("bg", [P, 8])
        ones = sb("ones", [P, 1])
        g_pre = sb("g_pre", [P, NC, 8])
        g_abs, g_e, lf = sb("g_abs", [P, 16]), sb("g_e", [P, 16]), sb("lf", [P, 16])
        b_cum = sb("b_cum", [P, 32])
        a_pad = sb("a_pad", [P, P])
        inter_row = silu_zp[0:16, 0:P]
        aT, cmax, mp_diag = silu_zp[0:16, 0:P], silu_zp[0:16, P:2 * P], silu_zp[0:16, 2 * P:2 * P + 16]
        diag = sb("diag", [P, 16])
        m_prev, m_last = sb("m_prev", [P, 20]), sb("m_last", [P, 16])
        mp_col = sb("mp_col", [16, 1])
        m_row = sb("m_row", [P, P])
        m_hl, inter_hl = sb("m_hl", [P, P], F32R), sb("inter_hl", [P, P], F32R)
        row_sel = sb("row_sel", [P, 16], F32R)
        expo = sb("expo", [P, 3, 16])
        den, rden = sb("den", [P, NH]), sb("rden", [P, NH])
        h_sq, h_var, h_rs = sb("h_sq", [P, NH]), sb("h_var", [P, NH]), sb("h_rs", [P, NH])
        x_sq, x_var, x_rs = sb("x_sq", [P, 2]), sb("x_var", [P, 2]), sb("x_rs", [P, 2])
        o_sq, o_var, o_rs = sb("o_sq", [P, 2]), sb("o_var", [P, 2]), sb("o_rs", [P, 2])
        mhalf = sb("mhalf", [P, NH])

        acc = [bank("acc0"), bank("acc1")]
        sco = bank("sco")
        bro = bank("bro")
        num = [bank("num0"), bank("num1")]
        kv = [bank("kv0"), bank("kv1")]
        v_bank = [kv[0], kv[1], num[0], num[1]]

        ident, tri, bigm = cst[:, K_ID:K_ID + P], cst[:, K_TRI:K_TRI + P], cst[:, K_BIG:K_BIG + P]

        cst_loaded, par_loaded, misc_loaded = sem("cst_loaded"), sem("par_loaded"), sem("misc_loaded")
        rows_zeroed, mhalf_ready = sem("rows_zeroed"), sem("mhalf_ready")
        fg_loaded, wg_loaded = sem("fg_loaded"), sem("wg_loaded")
        ada_loaded = [sem(f"ada_loaded{i}") for i in range(3)]
        ada_summed, ada_used = sem("ada_summed"), sem("ada_used")
        gate_step, gate_summed = sem("gate_step"), sem("gate_summed")
        wout_loaded = [sem(f"wout_loaded{i}") for i in range(2)]
        wout_scaled, wout_hi_done, wout_lo_done = sem("wout_scaled"), sem("wout_hi_done"), sem("wout_lo_done")
        w_loaded = [sem(f"w_loaded{i}") for i in range(RING)]
        w_hi_done, w_lo_done, w_used = sem("w_hi_done"), sem("w_lo_done"), sem("w_used")
        wg_hi_done, wg_lo_done = sem("wg_hi_done"), sem("wg_lo_done")
        par_T, par_ready, c_tanh, silu_c_ready = sem("par_T"), sem("par_ready"), sem("c_tanh"), sem("silu_c_ready")
        gate_bc = sem("gate_bc")
        setup_done = sem("setup_done")
        x_loaded = [sem("x_loaded0"), sem("x_loaded1")]
        x_sq_done, x_var_done, x_rs_done, x_scaled = sem("x_sq_done"), sem("x_var_done"), sem("x_rs_done"), sem("x_scaled")
        x_T, h_full, h_hi, h_lo = sem("x_T"), sem("h_full"), sem("h_hi"), sem("h_lo")
        gates_done, gates_T, g_rows_ready, g_abs_done, g_ln_done, lf_ready = sem("gates_done"), sem("gates_T"), sem("g_rows_ready"), sem("g_abs_done"), sem("g_ln_done"), sem("lf_ready")
        g_exp_done = sem("g_exp_done")
        a_ready, diag_ready, m_ready = sem("a_ready"), sem("diag_ready"), sem("m_ready")
        inter_row_ready, expo_ready, expo_done = sem("inter_row_ready"), sem("expo_ready"), sem("expo_done")
        rows_hi, rows_lo = sem("rows_hi"), sem("rows_lo")
        bro_full, bro_free = sem("bro_full"), sem("bro_free")
        sco_full, sco_free = sem("sco_full"), sem("sco_free")
        acc_full = sem("acc_full")
        acc_free = [sem("acc_free0"), sem("acc_free1")]
        v_done, v_copied_act, v_copied_dve = sem("v_done"), sem("v_copied_act"), sem("v_copied_dve")
        shifted_free, conv_done = sem("shifted_free"), sem("conv_done")
        tanh_ready, qk_ready, o_tanh = sem("tanh_ready"), sem("qk_ready"), sem("o_tanh")
        pooled_ready, k_T, d_exp, k_w_ready = sem("pooled_ready"), sem("k_T"), sem("d_exp"), sem("k_w_ready")
        num_done, kv_done, h_ready, c_done = sem("num_done"), sem("kv_done"), sem("h_ready"), sem("c_done")
        h_sq_done, h_var_done, h_rs_done, hm_ready = sem("h_sq_done"), sem("h_var_done"), sem("h_rs_done"), sem("hm_ready")
        y_hi, y_lo, m_hi, m_lo = sem("y_hi"), sem("y_lo"), sem("m_hi"), sem("m_lo")
        res_loaded = [sem("res_loaded0"), sem("res_loaded1")]
        stored = [sem("stored0"), sem("stored1")]
        o_sq_done, o_var_done, o_rs_done, o_ready = (
            sem("o_sq_done"), sem("o_var_done"), sem("o_rs_done"), sem("o_ready"))
        dve_step = sem("dve_step")

        block = ctx.enter_context(nc.Block())

        gate_sum = x_in[:, 1, :]

        w_in_v = w_in[0].rearrange("(k p) n -> p k n", p=P)
        w_ada_v = w_ada[0].rearrange("(k p) n -> p k n", p=P)
        ada_buf = [t[:, :, :].rearrange("p h (a n) -> p (h a) n", n=256) for t in (qT, kT, oz)]

        def reach(eng, sem, value):
            if not (isinstance(value, int) and value <= 0):
                eng.wait_ge(sem, value)

        def chunk(j):
            return slice(P * j, P * j + P)

        def col(t, n, m=P):
            return t[:, n:n + 1].broadcast_to([P, m])

        @block.sync
        def _(sp):
            def load_w(b, m):
                if m >= RING or b is not None:
                    sp.wait_ge(w_lo_done, m - RING + 1 if b is None else b * UNITS + (m - RING + 1))
                n = m % UNITS
                if n < V_UNITS:
                    src, dst = w_in_v[:, n, OFF_V:OFF_V + 512], w_raw[:, m % RING, :]
                else:
                    name, i = TILES[(n - V_UNITS) // 2]
                    half = (n - V_UNITS) % 2
                    off = OFFSET[name] + P * i
                    src = w_in_v[:, 4 * half:4 * half + 4, off:off + P]
                    dst = w_raw[:, m % RING, :].rearrange("p (k n) -> p k n", n=P)
                sp.dma_start(dst, src).then_inc(w_loaded[m % RING], 16)

            def load_x(nb, c, setup=False):
                dst = x_in
                if not setup:
                    sp.wait_ge(x_T, nb * PREPS + (2 * c - 2))
                elif c >= 2:
                    sp.wait_ge(par_ready, 1)
                    sp.wait_ge(x_sq_done, c - 1)
                    dst = x_res
                sp.dma_start(dst[:, c % 2, :], x[0, bass.ds(nb * BLK + c * P, P), :]).then_inc(x_loaded[c % 2], 16)

            def load_res(b, j):
                reach(sp, stored[j % 2], 16 * (b * 2 + j // 2))
                sp.dma_start(x_res[:, j % 2, :], x[0, bass.ds(b * BLK + j * P, P), :]).then_inc(res_loaded[j % 2], 16)

            def store(b, j):
                sp.wait_ge(o_ready, b * NC + (j + 1))
                sp.dma_start(out[0, bass.ds(b * BLK + j * P, P), :], x_res[:, j % 2, :]).then_inc(stored[j % 2], 16)

            sp.dma_start(cst[:, :], consts[:, 0:K_END]).then_inc(cst_loaded, 16)
            sp.dma_start(warm[:, :, :].rearrange("p g n -> p (g n)"), consts[:, K_END:K_END + K_COR]).then_inc(misc_loaded, 16)
            rows = x_res[:, 0, 0:P]
            sp.wait_ge(rows_zeroed, 1)
            for at, src in ((C_NG, norm_g[0].rearrange("(t p) -> t p", p=P)), (C_C, c[0].rearrange("(t p) -> t p", p=P)),
                            (C_BA, b_ada[0].rearrange("(t p) -> t p", p=P)),
                            (C_CW, conv_w[0].rearrange("j (t p) -> (j t) p", p=P)),
                            (C_CB, conv_b[0].rearrange("(t p) -> t p", p=P)),
                            (C_LS, ls_pool[0].rearrange("(t p) -> t p", p=P)),
                            (C_MG, mh_norm_g[0].rearrange("(t p) -> t p", p=P))):
                sp.dma_start(rows[at:at + src.shape[0], :], src).then_inc(par_loaded, 16)

            def load_ada(g):
                if g == 11:
                    sp.wait_ge(gate_summed, 1)
                elif g >= 3:
                    sp.wait_ge(ada_used, g - 2)
                sp.dma_start(ada_buf[g % 3], w_ada_v[:, :, 256 * g:256 * g + 256]).then_inc(ada_loaded[g % 3], 16)

            def load_wout(k):
                if k >= 2:
                    sp.wait_ge(wout_lo_done, k - 1)
                sp.dma_start(x_res[:, k % 2, :], w_out[0, P * k:P * k + P, :]).then_inc(wout_loaded[k % 2], 16)

            for g in range(3):
                load_ada(g)
            load_x(0, 0, True)
            load_x(0, 1, True)
            for g in range(3, 8):
                load_ada(g)
                if g == 5:
                    load_x(0, 2, True)
                    load_x(0, 3, True)
            sp.dma_start(wg_raw[:, :, :], w_in_v[:, :, OFF_G:OFF_G + 8]).then_inc(wg_loaded, 16)
            sp.dma_start(bg[:, :], b_gates[0].partition_broadcast(P)).then_inc(misc_loaded, 16)
            for m in range(4):
                load_w(None, m)
            sp.dma_start(wpool[:, :, :], w_pool[0].rearrange("g c d -> c g d")).then_inc(misc_loaded, 16)
            for g in range(8, 11):
                load_ada(g)
            for m in range(4, 8):
                load_w(None, m)
            load_ada(11)
            sp.wait_ge(x_T, PREPS)
            load_wout(0)
            load_wout(1)
            sp.dma_start(fg[:, :], final_g.partition_broadcast(P)).then_inc(fg_loaded, 16)

            def one_block(b, last, first=False):
                wout_units = {V_UNITS + 2 * (WOUT_TILE + k) + 8: k for k in range(2, KT)} if first else {}
                for m in range(8, UNITS):
                    load_w(b, m)
                    if m in wout_units:
                        load_wout(wout_units[m])
                    if m == 44 and first:
                        sp.wait_ge(gate_bc, 1)
                    if m == (44 if first else 40) and not last:
                        load_x(b + 1, 0)
                        load_x(b + 1, 1)
                    if m == 48:
                        if first:
                            sp.wait_ge(wout_lo_done, KT)
                        load_res(b, 0)
                        load_res(b, 1)
                if not last:
                    for m in range(UNITS, UNITS + 4):
                        load_w(b, m)
                    load_x(b + 1, 2)
                store(b, 0)
                if not last:
                    load_w(b, UNITS + 4)
                    load_w(b, UNITS + 5)
                    load_x(b + 1, 3)
                load_res(b, 2)
                store(b, 1)
                load_res(b, 3)
                if not last:
                    load_w(b, UNITS + 6)
                    load_w(b, UNITS + 7)
                store(b, 2)
                store(b, 3)

            one_block(0, False, True)
            with sp.Fori(1, NB - 1) as b:
                one_block(b, False)
            one_block(NB - 1, True)
            for i in range(2):
                sp.wait_ge(stored[i], 16 * 2 * NB)

        @block.tensor
        def _(pe):
            def split3(dst, st_hi, st_lo, mv_hi, mv_lo, start, stop):
                pe.matmul(dst, st_hi, mv_hi, start=start, stop=False)
                pe.matmul(dst, st_hi, mv_lo, start=False, stop=False)
                return pe.matmul(dst, st_lo, mv_hi, start=False, stop=stop)

            def prep(nb, p, src=x_in):
                c, half = p // 2, p % 2
                if half == 0:
                    pe.wait_ge(x_scaled, nb * NC + (c + 1))
                if p >= 2:
                    pe.wait_ge(h_full, nb * PREPS + (p - 1))
                for i in range(4):
                    k = 4 * half + i
                    last = pe.transpose(num[p % 2][:, chunk(i)], src[:, c % 2, chunk(k)], ident)
                last.then_inc(x_T, 1)

            pe.wait_ge(cst_loaded, 16)
            pe.wait_ge(par_loaded, 16 * 7)
            pe.transpose(kv[0][:, 0:P], x_res[:, 0, 0:P], ident).then_inc(par_T, 1)

            def ada(g):
                pe.wait_ge(ada_summed, g + 1)
                if g == 0:
                    pe.wait_ge(par_ready, 1)
                for t in range(2):
                    last = pe.matmul(kv[1][:, 2 * g + t:2 * g + t + 1], ada_buf[g % 3][:, 0, chunk(t)], ones[:, :],
                                     start=True, stop=True)
                last.then_inc(ada_used, 1)

            def gate_broadcast():
                pe.wait_ge(gate_summed, 4)
                pe.wait_ge(v_copied_act, 1)
                for n in range(KT):
                    dst = kv[n // 4][:, chunk(n % 4)]
                    pe.matmul(dst, col(par, C_BA + 2 * KT + n), ident, start=True, stop=False)
                    last = pe.matmul(dst, col(ones, 0), gate_sum[:, chunk(n)], start=False, stop=True)
                last.then_inc(gate_bc, 1)

            for g in range(8):
                ada(g)
                if g == 6:
                    prep(0, 0)
                    prep(0, 1)
            for p in range(2, PREPS):
                prep(0, p, x_in if p < 4 else x_res)
            pe.wait_ge(setup_done, 1)

            def one_block(b, last_block, first=False):
                def acc_wait(name, i):
                    t = TASK[name, i]
                    reach(pe, acc_free[t % 2], b * (TASKS // 2) + t // 2)
                    return acc[t % 2]

                def tile(name, i):
                    dst = acc_wait(name, i)
                    for half in range(2):
                        m = unit0(name, i) + half
                        pe.wait_ge(w_lo_done, b * UNITS + (m + 1))
                        for k in range(4):
                            kk = 4 * half + k
                            last = split3(dst[:, :], w_hi[:, m % RING, chunk(k)], w_lo[:, m % RING, chunk(k)],
                                          hT_hi[:, kk, :], hT_lo[:, kk, :], kk == 0, kk == KT - 1)
                        if half == 0:
                            last.then_inc(w_used, 1)
                        else:
                            last.then_inc(acc_full, 1)

                def bro_wait(u):
                    reach(pe, bro_free, b * B_USES + u)

                def v_part(k, chunks):
                    pe.wait_ge(w_lo_done, b * UNITS + (k + 1))
                    for j in chunks:
                        last = split3(v_bank[j][:, :], hT_hi[:, k, chunk(j)], hT_lo[:, k, chunk(j)],
                                      w_hi[:, k % RING, :], w_lo[:, k % RING, :], k == 0, k == KT - 1)
                    return last

                pe.wait_ge(h_lo, b * PREPS + PREPS // 2)
                reach(pe, c_done, b * NC)
                for k in range(RING):
                    v_part(k, (0, 1))
                pe.wait_ge(h_lo, b * PREPS + PREPS)
                pe.wait_ge(wg_lo_done, 1)
                reach(pe, sco_free, b * S_USES)
                for k in range(KT):
                    last = split3(sco[0:8, :], wg_hi[:, k, :], wg_lo[:, k, :], hT_hi[:, k, :], hT_lo[:, k, :],
                                  k == 0, k == KT - 1)
                last.then_inc(gates_done, 1)
                pe.wait_ge(h_full, b * PREPS + PREPS)
                for k in range(V_UNITS):
                    last = v_part(k, (2, 3) if k < RING else range(NC))
                    last.then_inc(w_used if k < KT - 1 else v_done, 1)
                    if k == 1:
                        pe.wait_ge(g_rows_ready, b + 1)
                        for j in range(NC):
                            last = pe.transpose(sco[:, chunk(j)], silu_zp[:, chunk(j)], ident)
                        last.then_inc(gates_T, 1)
                    if k == 4:
                        bro_wait(0)
                        pe.wait_ge(lf_ready, b + 1)
                        pe.matmul(bro[:, 0:16], tri, lf[:, :], start=True, stop=True)
                        pe.matmul(bro[:, 16:32], col(ones, 0), lf[:, :], start=True, stop=True).then_inc(bro_full, 1)
                    if k == 5:
                        bro_wait(1)
                        pe.wait_ge(a_ready, b + 1)
                        pe.transpose(bro[:, chunk(0)], a_pad[:, :], ident).then_inc(bro_full, 1)
                    if k == 6:
                        bro_wait(2)
                        pe.wait_ge(diag_ready, b + 1)
                        pe.matmul(bro[:, 0:16], col(ones, 0), diag[:, :], start=True, stop=True).then_inc(bro_full, 1)
                bro_wait(3)
                pe.wait_ge(m_ready, b + 1)
                pe.transpose(bro[:, chunk(0)], m_row[:, :], ident).then_inc(bro_full, 1)

                for t, (name, i) in enumerate(TILES[:16]):
                    tile(name, i)
                    if t == 1 and first:
                        gate_broadcast()

                def heads_to_scores(j):
                    if j == 0:
                        pe.wait_ge(qk_ready, b * 8 + 8)
                        pe.wait_ge(v_copied_act, b + 1)
                        pe.wait_ge(v_copied_dve, b + 1)
                        pe.wait_ge(rows_lo, b + 1)
                    reach(pe, sco_free, b * S_USES + SCO["qk", j])
                    for h in range(NH):
                        last = pe.matmul(sco[:, chunk(h)], kT[:, h, chunk(j)], qT[:, h, chunk(j)], start=True, stop=True)
                    last.then_inc(sco_full, 1)
                    bro_wait(4 + 2 * j)
                    for h in range(NH):
                        last = pe.matmul(bro[:, chunk(h)], col(row_sel, NH * j + h), m_hl[:, :], start=True, stop=True)
                    last.then_inc(bro_full, 1)

                def keys_transposed(j):
                    if first and j == 0:
                        pe.wait_ge(wout_scaled, KT)
                    reach(pe, c_done, b * NC + j)
                    for h in range(NH):
                        last = pe.transpose(kv[1][:, chunk(h)], kT[:, h, chunk(j)], ident)
                    last.then_inc(k_T, 1)

                def inter_rows(j):
                    bro_wait(5 + 2 * j)
                    for h in range(NH):
                        last = pe.matmul(bro[:, chunk(h)], col(row_sel, NH * j + h), inter_hl[:, :],
                                         start=True, stop=True)
                    last.then_inc(bro_full, 1)

                def numerator_and_update(j):
                    pe.wait_ge(sco_free, b * S_USES + (SCO["qk", j] + 1))
                    pe.wait_ge(bro_free, b * B_USES + (6 + 2 * j))
                    reach(pe, h_ready, b * NC + j)
                    for h in range(NH):
                        dst = num[h // 2][:, 129 * (h % 2):129 * (h % 2) + 129]
                        pe.matmul(dst, dmat[:, h, :], v[:, j, h, :], start=True, stop=False)
                        last = pe.matmul(dst, q_in[:, h, :], cmem[:, h, :], start=False, stop=True)
                    last.then_inc(num_done, 1)
                    pe.wait_ge(k_w_ready, b * NC + (j + 1))
                    for h in range(NH):
                        last = pe.matmul(kv[h // 2][:, 129 * (h % 2):129 * (h % 2) + 129], k_w[:, h, :], v[:, j, h, :],
                                         start=True, stop=True)
                    last.then_inc(kv_done, 1)

                def pool_map(g):
                    dst = acc_wait("y", g)
                    pe.wait_ge(pooled_ready, b * NH + (g + 1))
                    pe.matmul(dst[:, :], wpool[:, g, :], acc_cv[:, HALO:], start=True, stop=True).then_inc(acc_full, 1)

                def hm_transposed(j):
                    pe.wait_ge(sco_free, b * S_USES + SCO["hm", j])
                    pe.wait_ge(hm_ready, b * NC + (j + 1))
                    for h in range(NH):
                        last = pe.transpose(sco[:, chunk(h)], hm[:, h, :], ident)
                    last.then_inc(sco_full, 1)

                for j in range(NC):
                    heads_to_scores(j)
                    tile("u", j)
                    keys_transposed(j)
                    if j > 0:
                        pool_map(j - 1)
                        hm_transposed(j - 1)
                    inter_rows(j)
                    tile("zp", j)
                    numerator_and_update(j)
                pool_map(3)

                def out_m(i):
                    j, cols = i // 2, slice(512 * (i % 2), 512 * (i % 2) + 512)
                    dst = acc_wait("out", i)
                    if first and i == 0:
                        pe.wait_ge(wout_lo_done, KT)
                    if i % 2 == 0:
                        pe.wait_ge(m_lo, b * NC + (j + 1))
                    for h in range(NH):
                        split3(dst[:, :], mixm_hi[:, j % 2, h, :], mixm_lo[:, j % 2, h, :],
                               wo_hi[:, NH + h, cols], wo_lo[:, NH + h, cols], h == 0, False)

                def out_p(i):
                    j, cols = i // 2, slice(512 * (i % 2), 512 * (i % 2) + 512)
                    dst = acc[TASK["out", i] % 2]
                    if i == 0:
                        pe.wait_ge(y_lo, b * NH + NH)
                    for g in range(NH):
                        last = split3(dst[:, :], mixp_hi[:, g, chunk(j)], mixp_lo[:, g, chunk(j)],
                                      wo_hi[:, g, cols], wo_lo[:, g, cols], False, g == NH - 1)
                    last.then_inc(acc_full, 1)

                def prep_next(p):
                    if not last_block:
                        if p == 0:
                            pe.wait_ge(h_ready, b * NC + NC)
                        prep(b + 1, p)

                out_m(0)
                prep_next(0)
                prep_next(1)
                out_m(1)
                for i in range(8):
                    if i > 1:
                        out_m(i)
                    out_p(i)
                    if i == 1:
                        hm_transposed(3)
                    if i in (2, 4, 6):
                        prep_next(i)
                        prep_next(i + 1)

            one_block(0, False, True)
            with pe.Fori(1, NB - 1) as b:
                one_block(b, False)
            one_block(NB - 1, True)

        @block.scalar
        def _(act):
            def split_w(b, m):
                if b is None:
                    act.wait_ge(w_loaded[m % RING], 16)
                else:
                    act.wait_ge(w_loaded[m % RING], 16 * (b * WU + (m // RING + 1)))
                    used_wait(b, m - RING)
                act.activation(w_hi[:, m % RING, :], w_raw[:, m % RING, :], ACT.Copy).then_inc(w_hi_done, 1)

            def used_wait(b, m):
                if m < V_UNITS - 1:
                    act.wait_ge(w_used, b * 31 + (m + 1))
                elif m == V_UNITS - 1:
                    act.wait_ge(v_done, b + 1)
                else:
                    t, half = divmod(m - V_UNITS, 2)
                    if half == 0:
                        act.wait_ge(w_used, b * 31 + (V_UNITS - 1 + t + 1))
                    else:
                        act.wait_ge(acc_full, b * TASKS + (TASK[TILES[t]] + 1))

            def prep_sq(nb, c, src=x_in):
                act.wait_ge(x_loaded[c % 2], 16 * (nb * 2 + (c // 2 + 1)))
                act.activation(junk, src[:, c % 2, :], ACT.Square,
                               accum_out=x_sq[:, c % 2:c % 2 + 1]).then_inc(x_sq_done, 1)

            def prep_hi(nb, p):
                act.wait_ge(h_full, nb * PREPS + (p + 1))
                act.activation(hT_hi[:, 4 * (p % 2):4 * (p % 2) + 4, chunk(p // 2)], full[p % 2][:, :, :],
                               ACT.Copy).then_inc(h_hi, 1)

            act.wait_ge(par_ready, 1)
            act.activation(tanh[:, 0:KT], par[:, C_C:C_C + KT], ACT.Tanh, scale=0.5).then_inc(c_tanh, 1)
            act.wait_ge(silu_c_ready, 1)
            prep_sq(0, 0)
            act.wait_ge(x_sq_done, 1)
            prep_sq(0, 1)
            for c in range(2, NC):
                act.wait_ge(x_sq_done, c)
                act.wait_ge(x_var_done, c - 1)
                prep_sq(0, c, x_res)
            act.wait_ge(wg_loaded, 16)
            act.activation(wg_hi[:, :, :], wg_raw[:, :, :], ACT.Copy).then_inc(wg_hi_done, 1)
            for m in range(4):
                split_w(None, m)
            for p in range(PREPS):
                prep_hi(0, p)

            def wout_high(k):
                act.wait_ge(wout_scaled, k + 1)
                act.activation(wo_hi[:, k, :], x_res[:, k % 2, :], ACT.Copy).then_inc(wout_hi_done, 1)

            def one_block(b, last_block, first=False):
                def acc_wait(name, i):
                    t = TASK[name, i]
                    act.wait_ge(acc_full, b * TASKS + (t + 1))
                    return acc[t % 2], acc_free[t % 2]

                def tanh_wait(n):
                    if n == 0:
                        act.wait_ge(x_sq_done, b * NC + NC)
                        reach(act, o_sq_done, b * NC)
                        return
                    name, i = TANH_TILES[n - 1]
                    if name in "qk":
                        act.wait_ge(qk_ready, b * 8 + n)
                    else:
                        t = TASK[name, i]
                        act.wait_ge(acc_free[t % 2], b * (TASKS // 2) + (t // 2 + 1))

                act.wait_ge(g_abs_done, b + 1)
                act.activation(g_e[:, :], g_abs[:, :], ACT.Exp, scale=-1.0).then_inc(g_exp_done, 1)
                act.wait_ge(g_exp_done, b + 1)
                act.activation(g_e[:, :], g_e[:, :], ACT.Ln, bias=1.0).then_inc(g_ln_done, 1)
                for m in range(4, 10):
                    split_w(b, m)
                act.wait_ge(m_ready, b + 1)
                act.activation(inter_row, m_row[0:16, :], ACT.Exp, scale=-1.0,
                               bias=mp_col[:, :]).then_inc(inter_row_ready, 1)
                act.activation(m_hl[0:16, :], m_row[0:16, :], ACT.Copy)
                act.wait_ge(inter_row_ready, b + 1)
                act.activation(inter_hl[0:16, :], inter_row, ACT.Copy).then_inc(rows_hi, 1)
                split_w(b, 10)
                act.wait_ge(v_done, b + 1)
                for j in range(2):
                    last = act.activation(v[:, j, :, 0:P], v_bank[j][:, :].rearrange("p (h d) -> p h d", d=P), ACT.Copy)
                last.then_inc(v_copied_act, 1)
                split_w(b, 11)
                act.wait_ge(expo_ready, b + 1)
                act.activation(expo[:, :, :], expo[:, :, :], ACT.Exp, scale=-1.0).then_inc(expo_done, 1)

                for t, (name, i) in enumerate(TILES[:16]):
                    m = V_UNITS + 2 * t + 4
                    split_w(b, m)
                    src, free = acc_wait(name, i)
                    if name in "qk":
                        if t > 1:
                            act.wait_ge(shifted_free, b * 8 + (t - 1))
                        else:
                            reach(act, pooled_ready, b * NH)
                        act.activation(shifted[:, t % 2, HALO:], src[:, :], ACT.Copy).then_inc(free, 1)
                        split_w(b, m + 1)
                        act.wait_ge(conv_done, b * 8 + (t + 1))
                        tanh_wait(t)
                        act.activation(tanh[:, :], acc_cv[:, HALO:], ACT.Tanh, scale=0.5).then_inc(tanh_ready, 1)
                        if first and t > WOUT_TILE:
                            wout_high(t - WOUT_TILE - 1)
                    else:
                        tanh_wait(t)
                        if name == "z":
                            act.activation(tanh[:, :], src[:, :], ACT.Tanh, scale=0.5).then_inc(tanh_ready, 1)
                        else:
                            act.activation(tanh[:, :], src[:, :], ACT.Tanh, scale=0.5).then_inc(o_tanh, 1)
                            act.wait_ge(o_tanh, b * NH + (i + 1))
                            act.activation(tanh[:, :], tanh[:, :], ACT.Identity, scale=mg4[:, i:i + 1],
                                           bias=mg4[:, i:i + 1]).then_inc(tanh_ready, 1)
                        split_w(b, m + 1)
                        if first and t - WOUT_TILE - 1 < KT:
                            wout_high(t - WOUT_TILE - 1)

                def squares(j):
                    act.wait_ge(h_ready, b * NC + (j + 1))
                    for h in range(NH):
                        last = act.activation(junk[:, chunk(h)], hm[:, h, :], ACT.Square, accum_out=h_sq[:, h:h + 1])
                    last.then_inc(h_sq_done, 1)

                def y_high(g):
                    t = TASK["y", g]
                    act.wait_ge(acc_free[t % 2], b * (TASKS // 2) + (t // 2 + 1))
                    act.activation(mixp_hi[:, g, :], silu_zp[:, :], ACT.Copy).then_inc(y_hi, 1)

                def m_high(j):
                    act.wait_ge(sco_free, b * S_USES + (SCO["hm", j] + 1))
                    if j >= 2:
                        act.wait_ge(acc_full, b * TASKS + (TASK["out", 2 * j - 3] + 1))
                    act.activation(mixm_hi[:, j % 2, :, :], oz[:, :, chunk(j)], ACT.Copy).then_inc(m_hi, 1)

                for j in range(NC):
                    m = unit0("u", j) + 4
                    if j > 0:
                        squares(j - 1)
                    act.wait_ge(bro_free, b * B_USES + (5 + 2 * j))
                    act.activation(dmat[:, :, :], dmat[:, :, :], ACT.Exp, scale=-1.0).then_inc(d_exp, 1)
                    if not last_block or m < UNITS:
                        split_w(b, m)
                    src, free = acc_wait("u", j)
                    if j > 0:
                        act.wait_ge(pooled_ready, b * NH + j)
                    else:
                        act.wait_ge(shifted_free, b * 8 + 8)
                    act.activation(shifted[:, 0, HALO:], src[:, :], ACT.Copy).then_inc(free, 1)
                    if not last_block or m < UNITS:
                        split_w(b, m + 1)
                    if j > 0:
                        y_high(j - 1)
                    if j >= 2:
                        m_high(j - 2)
                    if not last_block or m + 2 < UNITS:
                        split_w(b, m + 2)
                    reach(act, h_sq_done, b * NC + j)
                    if j >= 2 and not last_block:
                        prep_sq(b + 1, j - 2)
                        act.wait_ge(x_sq_done, (b + 1) * NC + (j - 1))
                    src, free = acc_wait("zp", j)
                    tanh_wait(16 + j)
                    act.activation(tanh[:, :], src[:, :], ACT.Tanh, scale=0.5).then_inc(tanh_ready, 1)
                    if not last_block or m + 2 < UNITS:
                        split_w(b, m + 3)

                def out_sq(j):
                    t = TASK["out", 2 * j + 1]
                    act.wait_ge(acc_free[t % 2], b * (TASKS // 2) + (t // 2 + 1))
                    if j == 0:
                        act.wait_ge(h_sq_done, b * NC + NC)
                    elif j < 3 and not last_block:
                        act.wait_ge(x_sq_done, (b + 1) * NC + (j + 2))
                    else:
                        act.wait_ge(o_sq_done, b * NC + j)
                    act.activation(junk, x_res[:, j % 2, :], ACT.Square,
                                   accum_out=o_sq[:, j % 2:j % 2 + 1]).then_inc(o_sq_done, 1)

                squares(3)
                y_high(3)
                for i in range(8):
                    if i % 2 == 0 and not last_block:
                        prep_hi(b + 1, i)
                        prep_hi(b + 1, i + 1)
                    if i % 2:
                        out_sq(i // 2)
                    if i in (1, 3) and not last_block:
                        act.wait_ge(o_sq_done, b * NC + (i // 2 + 1))
                        prep_sq(b + 1, 2 + i // 2)
                    if i in (1, 3):
                        m_high(2 + i // 2)

            one_block(0, False, True)
            with act.Fori(1, NB - 1) as b:
                one_block(b, False)
            one_block(NB - 1, True)

        @block.gpsimd
        def _(pool):
            def low_w(b, m):
                pool.wait_ge(w_hi_done, m + 1 if b is None else b * UNITS + (m + 1))
                nc.gpsimd.tensor_tensor(w_lo[:, m % RING, :], w_raw[:, m % RING, :], w_hi[:, m % RING, :].bitcast(F32),
                                        ALU.subtract).then_inc(w_lo_done, 1)

            def prep_lo(nb, p):
                pool.wait_ge(h_hi, nb * PREPS + (p + 1))
                dst = slice(4 * (p % 2), 4 * (p % 2) + 4), chunk(p // 2)
                nc.gpsimd.tensor_tensor(hT_lo[:, dst[0], dst[1]], full[p % 2][:, :, :], hT_hi[:, dst[0], dst[1]].bitcast(F32),
                                        ALU.subtract).then_inc(h_lo, 1)

            def rsqrt(var_done, value, dst, src, done):
                n = src.shape[1]
                pool.wait_ge(var_done, value)
                nc.gpsimd.tensor_tensor(dst, src, mhalf[:, 0:n], ALU.pow).then_inc(done, 1)

            def x_rsqrt(nb, c):
                rsqrt(x_var_done, nb * NC + (c + 1), x_rs[:, c % 2:c % 2 + 1], x_var[:, c % 2:c % 2 + 1], x_rs_done)

            nc.gpsimd.memset(mhalf[:, :], -0.5).then_inc(mhalf_ready, 1)
            pool.wait_ge(mhalf_ready, 1)
            for c in range(NC):
                x_rsqrt(0, c)
            pool.wait_ge(wg_hi_done, 1)
            nc.gpsimd.tensor_tensor(wg_lo[:, :, :], wg_raw[:, :, :], wg_hi[:, :, :].bitcast(F32),
                                    ALU.subtract).then_inc(wg_lo_done, 1)
            for m in range(4):
                low_w(None, m)
            for p in range(PREPS):
                prep_lo(0, p)

            def one_block(b, last_block):
                def h_rsqrt(j):
                    rsqrt(h_var_done, b * NC + (j + 1), h_rs[:, :], h_var[:, :], h_rs_done)

                for m in range(4, 40):
                    low_w(b, m)
                for m0 in range(44, 60, 4):
                    j = (m0 - 44) // 4
                    if j == 0:
                        for m in range(40, 44):
                            low_w(b, m)
                    if j > 0:
                        h_rsqrt(j - 1)
                    for m in range(m0, m0 + 4):
                        if m < UNITS or not last_block:
                            low_w(b, m)
                        if m == m0 + 2 and j >= 2 and not last_block:
                            x_rsqrt(b + 1, j - 2)
                h_rsqrt(3)
                for i in range(8):
                    if i % 2 == 0 and not last_block:
                        prep_lo(b + 1, i)
                        prep_lo(b + 1, i + 1)
                    if i in (1, 3) and not last_block:
                        x_rsqrt(b + 1, 2 + i // 2)
                    if i % 2:
                        j = i // 2
                        rsqrt(o_var_done, b * NC + (j + 1), o_rs[:, j % 2:j % 2 + 1], o_var[:, j % 2:j % 2 + 1], o_rs_done)

            one_block(0, False)
            with pool.Fori(1, NB - 1) as b:
                one_block(b, False)
            one_block(NB - 1, True)

        @block.vector
        def _(dve):
            V = nc.vector
            count = [0]
            base = [0]
            latest = [None]

            def step(ins):
                ins.then_inc(dve_step, 1)
                count[0] += 1
                did(dve_step, base[0] + count[0])

            def did(sem, value):
                latest[0] = (sem, value)

            def in_turn():
                reach(dve, *latest[0])

            def prep_scale(nb, c, src=x_in):
                s = slice(c % 2, c % 2 + 1)
                in_turn()
                dve.wait_ge(x_rs_done, nb * NC + (c + 1))
                V.tensor_scalar(src[:, c % 2, :], src[:, c % 2, :], x_rs[:, s], None, ALU.mult).then_inc(x_scaled, 1)
                did(x_scaled, nb * NC + (c + 1))

            def prep_var(nb, c):
                s = slice(c % 2, c % 2 + 1)
                in_turn()
                dve.wait_ge(x_sq_done, nb * NC + (c + 1))
                V.tensor_scalar(x_var[:, s], x_sq[:, s], 1.0 / D, EPS, ALU.mult, ALU.add).then_inc(x_var_done, 1)
                did(x_var_done, nb * NC + (c + 1))

            def prep_full(nb, p, first=False):
                in_turn()
                dve.wait_ge(x_T, nb * PREPS + (p + 1))
                if not first:
                    dve.wait_ge(h_lo, nb * PREPS + (p - 1))
                for i in range(4):
                    k = 4 * (p % 2) + i
                    last = V.tensor_scalar(full[p % 2][:, i, :], num[p % 2][:, chunk(i)], gain[:, k:k + 1], shift[:, k:k + 1],
                                           ALU.mult, ALU.add)
                last.then_inc(h_full, 1)
                did(h_full, nb * PREPS + (p + 1))

            V.memset(x_res[:, 0, 0:P], 0.0).then_inc(rows_zeroed, 1)
            for t in (halo_qk[:, :, :], halo_u[:, :, :], cmem[:, :, :], a_pad[:, :], m_row[:, :],
                      diag[:, :], m_prev[:, :], silu_zp[:, :]):
                V.memset(t, 0.0)
            V.memset(ones[:, :], 1.0)
            for t in range(2):
                V.memset(shifted[:, t, :], 0.0)
            step(V.memset(v[:, :, :, P:P + 1], 1.0))
            in_turn()
            V.tensor_copy(m_hl[:, :], m_row[:, :])
            step(V.tensor_copy(inter_hl[:, :], m_row[:, :]))
            dve.wait_ge(par_T, 1)
            step(V.tensor_tensor(row_sel[:, :], ident[:, 0:16], ident[:, LO_ROW:LO_ROW + 16], ALU.add))
            V.tensor_copy(par[:, :], kv[0][:, 0:C_END]).then_inc(par_ready, 1)
            did(par_ready, 1)
            dve.wait_ge(par_ready, 1)
            dve.wait_ge(c_tanh, 1)
            step(V.scalar_tensor_tensor(silu_c[:, :], tanh[:, 0:KT], 1.0, par[:, C_C:C_C + KT], ALU.add, ALU.mult))
            in_turn()
            V.tensor_scalar(silu_c[:, :], silu_c[:, :], 0.5, None, ALU.mult).then_inc(silu_c_ready, 1)
            did(silu_c_ready, 1)
            V.tensor_scalar(mg4[:, :], par[:, C_MG:C_MG + NH], 0.25, None, ALU.mult)
            V.tensor_scalar(ls2[:, :], par[:, C_LS:C_LS + NH], 0.5, None, ALU.mult)

            def weighted_sum(g, last_dst, mark):
                buf = ada_buf[g % 3]
                in_turn()
                dve.wait_ge(ada_loaded[g % 3], 16 * (g // 3 + 1))
                mark(V.tensor_scalar(buf[:, 0, :], buf[:, 0, :], silu_c[:, 0:1], None, ALU.mult))
                for k in range(1, KT):
                    in_turn()
                    dst = buf[:, 0, :] if k < KT - 1 else last_dst
                    ins = V.scalar_tensor_tensor(dst, buf[:, k, :], silu_c[:, k:k + 1], buf[:, 0, :], ALU.mult, ALU.add)
                    if k < KT - 1:
                        mark(ins)
                return ins

            gate_count = [0]

            def gate_mark(ins):
                ins.then_inc(gate_step, 1)
                gate_count[0] += 1
                did(gate_step, gate_count[0])

            def sum_gate(n):
                weighted_sum(8 + n, gate_sum[:, 256 * n:256 * n + 256], gate_mark).then_inc(gate_summed, 1)
                did(gate_summed, n + 1)

            for g in range(8):
                weighted_sum(g, ada_buf[g % 3][:, 0, :], step).then_inc(ada_summed, 1)
                did(ada_summed, g + 1)
                c_next = {3: 0, 4: 1, 6: 2, 7: 3}.get(g)
                if c_next is not None:
                    prep_var(0, c_next)
                    prep_scale(0, c_next, x_in if c_next < 2 else x_res)
            in_turn()
            dve.wait_ge(ada_used, 8)
            step(V.tensor_tensor(shift[:, :], kv[1][:, 0:KT], par[:, C_BA:C_BA + KT], ALU.add))
            step(V.tensor_tensor(gain[:, :], kv[1][:, KT:2 * KT], par[:, C_BA + KT:C_BA + 2 * KT], ALU.add))
            in_turn()
            step(V.scalar_tensor_tensor(gain[:, :], gain[:, :], 1.0, par[:, C_NG:C_NG + KT], ALU.add, ALU.mult))
            in_turn()
            for p in range(PREPS):
                prep_full(0, p, p < 2)

            def wout_scale(k):
                in_turn()
                dve.wait_ge(gate_bc, 1)
                dve.wait_ge(wout_loaded[k % 2], 16 * (k // 2 + 1))
                for n in range(2):
                    s = slice(512 * n, 512 * n + 512)
                    last = V.tensor_tensor(x_res[:, k % 2, s], x_res[:, k % 2, s], kv[n][:, :], ALU.mult)
                last.then_inc(wout_scaled, 1)
                did(wout_scaled, k + 1)

            def wout_low(k):
                in_turn()
                dve.wait_ge(wout_hi_done, k + 1)
                V.tensor_tensor(wo_lo[:, k, :], x_res[:, k % 2, :], wo_hi[:, k, :].bitcast(F32),
                                ALU.subtract).then_inc(wout_lo_done, 1)
                did(wout_lo_done, k + 1)

            in_turn()
            dve.wait_ge(misc_loaded, 48)
            dve.wait_ge(wg_lo_done, 1)
            step(V.memset(den[:, :], 0.0))
            in_turn()
            V.memset(rden[:, :], 0.0).then_inc(setup_done, 1)
            dve.wait_ge(setup_done, 1)
            did(setup_done, 1)
            setup_steps = count[0]

            def one_block(b, last_block, first=False):
                count[0] = 0
                base[0] = b * DVE_STEPS + setup_steps

                def bro_read(u):
                    dve.wait_ge(bro_full, b * B_USES + (u + 1))

                def acc_wait(name, i):
                    t = TASK[name, i]
                    dve.wait_ge(acc_full, b * TASKS + (t + 1))
                    return acc[t % 2], acc_free[t % 2]

                if first:
                    sum_gate(0)
                    sum_gate(1)
                else:
                    did(o_ready, b * NC)
                in_turn()
                dve.wait_ge(gates_done, b + 1)
                V.tensor_copy(silu_zp[0:8, :], sco[0:8, :]).then_inc(g_rows_ready, 1)
                dve.wait_ge(gates_T, b + 1)
                V.tensor_tensor(g_pre[:, :, :], sco[:, :].rearrange("p (c g) -> p c g", g=P)[:, :, 0:8],
                                bg[:, :].unsqueeze(1).broadcast_to([P, NC, 8]), ALU.add).then_inc(sco_free, 1)
                dve.wait_ge(sco_free, b * S_USES + 1)
                g_i, g_f = g_pre[:, :, 0:NH], g_pre[:, :, NH:2 * NH]
                lf_v = lf[:, :].rearrange("p (c h) -> p c h", h=NH)
                V.scalar_tensor_tensor(g_abs[:, :].rearrange("p (c h) -> p c h", h=NH), g_f, -1.0, g_f, ALU.mult,
                                       ALU.max).then_inc(g_abs_done, 1)
                did(g_abs_done, b + 1)
                in_turn()
                dve.wait_ge(g_ln_done, b + 1)
                V.scalar_tensor_tensor(lf_v, g_f, 0.0, g_e[:, :].rearrange("p (c h) -> p c h", h=NH), ALU.min,
                                       ALU.subtract).then_inc(lf_ready, 1)
                did(lf_ready, b + 1)
                if first:
                    sum_gate(2)
                in_turn()
                bro_read(0)
                V.tensor_copy(b_cum[:, :], bro[:, 0:32]).then_inc(bro_free, 1)
                dve.wait_ge(bro_free, b * B_USES + 1)
                V.tensor_tensor(a_pad[:, 0:16].rearrange("p (c h) -> p c h", h=NH), g_i,
                                b_cum[:, 0:16].rearrange("p (c h) -> p c h", h=NH), ALU.subtract).then_inc(a_ready, 1)
                did(a_ready, b + 1)
                if first:
                    sum_gate(3)
                in_turn()
                bro_read(1)
                V.tensor_copy(aT, bro[0:16, chunk(0)]).then_inc(bro_free, 1)
                dve.wait_ge(bro_free, b * B_USES + 2)
                step(V.tensor_tensor_scan(cmax, aT, aT, -3.0e38, ALU.max, ALU.max))
                in_turn()
                V.tensor_scalar(diag[0:16, :], ident[0:16, 0:16], cmax[:, P - 1:P], None, ALU.mult).then_inc(diag_ready, 1)
                did(diag_ready, b + 1)
                in_turn()
                bro_read(2)
                for j in range(NC):
                    s, n = slice(NH * j, NH * j + NH), slice(NH * j + NH, NH * j + 2 * NH)
                    step(V.tensor_tensor(m_last[:, s], m_prev[:, s], bro[:, s], ALU.max))
                    in_turn()
                    ins = V.tensor_tensor(m_prev[:, n], m_last[:, s], b_cum[:, 16 + NH * j:16 + NH * j + NH], ALU.add)
                    if j < NC - 1:
                        step(ins)
                    else:
                        ins.then_inc(bro_free, 1)
                        did(bro_free, b * B_USES + 3)
                    in_turn()
                step(V.tensor_tensor(mp_diag, m_prev[0:16, 0:16], ident[0:16, 0:16], ALU.mult))
                in_turn()
                step(V.tensor_reduce(mp_col[:, :], mp_diag, AX.X, ALU.add))
                in_turn()
                V.tensor_scalar(m_row[0:16, :], cmax, mp_col[:, :], None, ALU.max).then_inc(m_ready, 1)
                did(m_ready, b + 1)
                step(V.tensor_tensor(expo[:, 1, :], m_last[:, :], a_pad[:, 0:16], ALU.subtract))
                step(V.tensor_tensor(expo[:, 2, :], m_last[:, :], m_prev[:, 0:16], ALU.subtract))
                bro_read(3)
                V.tensor_tensor(expo[:, 0, :], b_cum[:, 0:16], bro[:, 0:16], ALU.add).then_inc(bro_free, 1)
                dve.wait_ge(bro_free, b * B_USES + 4)
                V.tensor_copy(m_prev[:, 0:NH], m_prev[:, 16:20]).then_inc(expo_ready, 1)
                did(expo_ready, b + 1)
                in_turn()
                dve.wait_ge(v_done, b + 1)
                for j in range(2, 4):
                    last = V.tensor_copy(v[:, j, :, 0:P], v_bank[j][:, :].rearrange("p (h d) -> p h d", d=P))
                last.then_inc(v_copied_dve, 1)
                dve.wait_ge(rows_hi, b + 1)
                V.tensor_tensor(m_hl[LO_ROW:LO_ROW + 16, :], m_row[0:16, :], m_hl[0:16, :].bitcast(F32), ALU.subtract)
                V.tensor_tensor(inter_hl[LO_ROW:LO_ROW + 16, :], inter_row, inter_hl[0:16, :].bitcast(F32),
                                ALU.subtract).then_inc(rows_lo, 1)
                did(rows_lo, b + 1)

                for t, (name, i) in enumerate(TILES[:16]):
                    in_turn()
                    if name in "qk":
                        sh = shifted[:, t % 2, :]
                        tap = [par[:, C_CW + 8 * n + t:C_CW + 8 * n + t + 1] for n in range(CW)]
                        step(V.tensor_copy(sh[:, HALO - 3:HALO], halo_qk[:, t, :]))
                        dve.wait_ge(acc_free[t % 2], b * (TASKS // 2) + (t // 2 + 1))
                        step(V.tensor_scalar(acc_cv[:, HALO:], sh[:, HALO:], tap[3], par[:, C_CB + t:C_CB + t + 1],
                                             ALU.mult, ALU.add))
                        for n in (2, 1, 0):
                            in_turn()
                            ins = V.scalar_tensor_tensor(acc_cv[:, HALO:], sh[:, HALO - 3 + n:HALO - 3 + n + BLK], tap[n],
                                                         acc_cv[:, HALO:], ALU.mult, ALU.add)
                            if n:
                                step(ins)
                            else:
                                ins.then_inc(conv_done, 1)
                                did(conv_done, b * 8 + (t + 1))
                        V.tensor_copy(halo_qk[:, t, :], sh[:, HALO + BLK - 3:HALO + BLK]).then_inc(shifted_free, 1)
                        dve.wait_ge(tanh_ready, b * TANHS + (t + 1))
                        dve.wait_ge(conv_done, b * 8 + (t + 1))
                        V.scalar_tensor_tensor((qT if name == "q" else kT)[:, i, :], tanh[:, :], 1.0, acc_cv[:, HALO:],
                                               ALU.add, ALU.mult).then_inc(qk_ready, 1)
                        did(qk_ready, b * 8 + (t + 1))
                    elif name == "z":
                        src, free = acc_wait(name, i)
                        dve.wait_ge(tanh_ready, b * TANHS + (t + 1))
                        V.scalar_tensor_tensor(oz[:, i, :], tanh[:, :], 1.0, src[:, :], ALU.add, ALU.mult).then_inc(free, 1)
                        did(free, b * (TASKS // 2) + (TASK[name, i] // 2 + 1))
                    else:
                        src, free = acc_wait(name, i)
                        dve.wait_ge(tanh_ready, b * TANHS + (t + 1))
                        V.tensor_tensor(oz[:, i, :], tanh[:, :], oz[:, i, :], ALU.mult).then_inc(free, 1)
                        did(free, b * (TASKS // 2) + (TASK[name, i] // 2 + 1))
                    if first and t > WOUT_TILE and t - WOUT_TILE <= KT:
                        wout_low(t - WOUT_TILE - 1)
                    if first and 0 <= t - WOUT_TILE < KT:
                        wout_scale(t - WOUT_TILE)
                if first:
                    in_turn()
                    dve.wait_ge(fg_loaded, 16)

                def rows(t):
                    return t.unsqueeze(2).broadcast_to([P, t.shape[1], P])

                def heads(j):
                    in_turn()
                    dve.wait_ge(num_done, b * NC + (j + 1))
                    pairs = [t[:, 0:258].rearrange("p (h d) -> p h d", d=P + 1) for t in num]
                    for q in range(2):
                        n = slice(NH * j + 2 * q, NH * j + 2 * q + 2)
                        step(V.scalar_tensor_tensor(den[:, 2 * q:2 * q + 2].unsqueeze(2), pairs[q][:, :, P:P + 1], -1.0,
                                                    expo[:, 0, n].unsqueeze(2), ALU.mult, ALU.max))
                    in_turn()
                    for q in range(2):
                        step(V.tensor_tensor(den[:, 2 * q:2 * q + 2].unsqueeze(2), den[:, 2 * q:2 * q + 2].unsqueeze(2),
                                             pairs[q][:, :, P:P + 1], ALU.max))
                    in_turn()
                    step(V.reciprocal(rden[:, :], den[:, :]))
                    in_turn()
                    for q in range(2):
                        last = V.tensor_tensor(hm[:, 2 * q:2 * q + 2, :], pairs[q][:, :, 0:P], rows(rden[:, 2 * q:2 * q + 2]),
                                               ALU.mult)
                    last.then_inc(h_ready, 1)
                    did(h_ready, b * NC + (j + 1))

                def update_c(j):
                    in_turn()
                    dve.wait_ge(kv_done, b * NC + (j + 1))
                    for h in range(NH):
                        last = V.scalar_tensor_tensor(cmem[:, h, :], cmem[:, h, :], expo[:, 2, NH * j + h:NH * j + h + 1],
                                                      kv[h // 2][:, 129 * (h % 2):129 * (h % 2) + 129], ALU.mult, ALU.add)
                    last.then_inc(c_done, 1)
                    did(c_done, b * NC + (j + 1))

                def head_var(j):
                    in_turn()
                    dve.wait_ge(h_sq_done, b * NC + (j + 1))
                    V.tensor_scalar(h_var[:, :], h_sq[:, :], 1.0 / P, EPS, ALU.mult, ALU.add).then_inc(h_var_done, 1)
                    did(h_var_done, b * NC + (j + 1))

                def head_norm(j):
                    dve.wait_ge(h_rs_done, b * NC + (j + 1))
                    in_turn()
                    V.tensor_tensor(hm[:, :, :], hm[:, :, :], rows(h_rs[:, :]), ALU.mult).then_inc(hm_ready, 1)
                    did(hm_ready, b * NC + (j + 1))

                def y_mixed(g):
                    in_turn()
                    src, free = acc_wait("y", g)
                    V.scalar_tensor_tensor(silu_zp[:, :], src[:, :], ls2[:, g:g + 1], silu_zp[:, :], ALU.mult,
                                           ALU.mult).then_inc(free, 1)
                    did(free, b * (TASKS // 2) + (TASK["y", g] // 2 + 1))

                def y_low(g):
                    in_turn()
                    dve.wait_ge(y_hi, b * NH + (g + 1))
                    V.tensor_tensor(mixp_lo[:, g, :], silu_zp[:, :], mixp_hi[:, g, :].bitcast(F32),
                                    ALU.subtract).then_inc(y_lo, 1)
                    did(y_lo, b * NH + (g + 1))

                def m_mixed(j):
                    in_turn()
                    dve.wait_ge(sco_full, b * SCO_FULLS + SCO["hm", j])
                    V.tensor_tensor(oz[:, :, chunk(j)], sco[:, :].rearrange("p (h t) -> p h t", t=P), oz[:, :, chunk(j)],
                                    ALU.mult).then_inc(sco_free, 1)
                    did(sco_free, b * S_USES + (SCO["hm", j] + 1))

                def m_low(j):
                    in_turn()
                    dve.wait_ge(m_hi, b * NC + (j + 1))
                    V.tensor_tensor(mixm_lo[:, j % 2, :, :], oz[:, :, chunk(j)], mixm_hi[:, j % 2, :, :].bitcast(F32),
                                    ALU.subtract).then_inc(m_lo, 1)
                    did(m_lo, b * NC + (j + 1))

                def windows(g):
                    sh, levels = shifted[:, 0, :], g + 1
                    in_turn()
                    step(V.tensor_copy(sh[:, 0:HALO], halo_u[:, g, :]))
                    t = TASK["u", g]
                    dve.wait_ge(acc_free[t % 2], b * (TASKS // 2) + (t // 2 + 1))
                    src = sh
                    for n in range(levels):
                        dst, lo, by = (shifted[:, 1, :], acc_cv[:, :])[n % 2], 2 ** (n + 1) - 1, 2 ** n
                        in_turn()
                        step(V.tensor_tensor(dst[:, lo:], src[:, lo:], src[:, lo - by:HALO + BLK - by], ALU.add))
                        src = dst
                    in_turn()
                    step(V.tensor_tensor(src[:, HALO:HALO + 15], src[:, HALO:HALO + 15], warm[:, g, :], ALU.mult))
                    step(V.tensor_copy(halo_u[:, g, :], sh[:, BLK:]))
                    in_turn()
                    V.scalar_tensor_tensor(acc_cv[:, HALO:], src[:, HALO:], 1.0 / WINDOWS[g], sh[:, HALO:], ALU.mult,
                                           ALU.subtract).then_inc(pooled_ready, 1)
                    did(pooled_ready, b * NH + (g + 1))

                dve.wait_ge(expo_done, b + 1)
                for j in range(NC):
                    if j > 0:
                        heads(j - 1)
                        update_c(j - 1)
                    in_turn()
                    bro_read(4 + 2 * j)
                    for h in range(NH):
                        last = V.scalar_tensor_tensor(dmat[:, h, :], bro[:, chunk(h)], a_pad[:, NH * j + h:NH * j + h + 1],
                                                      bigm, ALU.subtract, ALU.add)
                    last.then_inc(bro_free, 1)
                    did(bro_free, b * B_USES + (5 + 2 * j))
                    in_turn()
                    dve.wait_ge(sco_full, b * SCO_FULLS + SCO["qk", j])
                    dve.wait_ge(d_exp, b * NC + (j + 1))
                    V.scalar_tensor_tensor(dmat[:, :, :].rearrange("p h t -> p (h t)"), sco[:, :], QK_SCALE,
                                           dmat[:, :, :].rearrange("p h t -> p (h t)"), ALU.mult,
                                           ALU.mult).then_inc(sco_free, 1)
                    did(sco_free, b * S_USES + (SCO["qk", j] + 1))
                    if j > 0:
                        head_var(j - 1)
                        head_norm(j - 1)
                        y_mixed(j - 1)
                        m_mixed(j - 1)
                    in_turn()
                    bro_read(5 + 2 * j)
                    V.scalar_tensor_tensor(q_in[:, :, :], qT[:, :, chunk(j)], QK_SCALE,
                                           bro[:, :].rearrange("p (h t) -> p h t", t=P), ALU.mult,
                                           ALU.mult).then_inc(bro_free, 1)
                    did(bro_free, b * B_USES + (6 + 2 * j))
                    dve.wait_ge(k_T, b * NC + (j + 1))
                    V.tensor_tensor(k_w[:, :, :], kv[1][:, :].rearrange("p (h d) -> p h d", d=P),
                                    rows(expo[:, 1, NH * j:NH * j + NH]), ALU.mult).then_inc(k_w_ready, 1)
                    did(k_w_ready, b * NC + (j + 1))
                    windows(j)
                    if j > 0:
                        y_low(j - 1)
                    if j >= 2:
                        m_low(j - 2)
                    if j >= 2 and not last_block:
                        prep_var(b + 1, j - 2)
                    in_turn()
                    src, free = acc_wait("zp", j)
                    dve.wait_ge(tanh_ready, b * TANHS + (17 + j))
                    V.scalar_tensor_tensor(silu_zp[:, :], tanh[:, :], 1.0, src[:, :], ALU.add, ALU.mult).then_inc(free, 1)
                    did(free, b * (TASKS // 2) + (TASK["zp", j] // 2 + 1))
                    if j >= 2 and not last_block:
                        prep_scale(b + 1, j - 2)

                def add_residual(i):
                    j, s = i // 2, slice(512 * (i % 2), 512 * (i % 2) + 512)
                    in_turn()
                    src, free = acc_wait("out", i)
                    if i % 2 == 0:
                        dve.wait_ge(res_loaded[j % 2], 16 * (b * 2 + (j // 2 + 1)))
                    V.tensor_tensor(x_res[:, j % 2, s], src[:, :], x_res[:, j % 2, s], ALU.add).then_inc(free, 1)
                    did(free, b * (TASKS // 2) + (TASK["out", i] // 2 + 1))

                def out_var(j):
                    s = slice(j % 2, j % 2 + 1)
                    in_turn()
                    dve.wait_ge(o_sq_done, b * NC + (j + 1))
                    V.tensor_scalar(o_var[:, s], o_sq[:, s], 1.0 / D, EPS, ALU.mult, ALU.add).then_inc(o_var_done, 1)
                    did(o_var_done, b * NC + (j + 1))

                def out_norm(j):
                    in_turn()
                    dve.wait_ge(o_rs_done, b * NC + (j + 1))
                    V.scalar_tensor_tensor(x_res[:, j % 2, :], x_res[:, j % 2, :], o_rs[:, j % 2:j % 2 + 1], fg[:, :],
                                           ALU.mult, ALU.mult).then_inc(o_ready, 1)
                    did(o_ready, b * NC + (j + 1))

                in_turn()
                step(V.memset(warm[:, :, :], 1.0))
                heads(3)
                update_c(3)
                y_mixed(3)
                head_var(3)
                y_low(3)
                head_norm(3)
                for i in range(8):
                    add_residual(i)
                    if i % 2 == 0 and not last_block:
                        prep_full(b + 1, i)
                        prep_full(b + 1, i + 1)
                    if i in (2, 4, 6):
                        out_norm(i // 2 - 1)
                    if i in (1, 3) and not last_block:
                        prep_var(b + 1, 2 + i // 2)
                    if i % 2:
                        out_var(i // 2)
                    if i == 1:
                        m_mixed(3)
                    if i in (1, 3):
                        m_low(2 + i // 2)
                    if i in (1, 3) and not last_block:
                        prep_scale(b + 1, 2 + i // 2)
                out_norm(3)
                assert count[0] == DVE_STEPS, count[0]

            one_block(0, False, True)
            with dve.Fori(1, NB - 1) as b:
                one_block(b, False)
            one_block(NB - 1, True)


INPUTS = ("x", "c", "norm_g", "w_ada", "b_ada", "w_in", "b_gates", "conv_w", "conv_b", "w_pool", "ls_pool",
          "mh_norm_g", "w_out", "final_g")


def constants():
    s, t = np.arange(P)[:, None], np.arange(P)[None, :]
    cor = [w / np.minimum(np.arange(1, 16), w) for w in WINDOWS]
    parts = [np.eye(P), s <= t, np.where(s > t, BIG, 0.0), np.tile(np.concatenate(cor), (P, 1))]
    return np.concatenate([np.asarray(a, np.float32) for a in parts], axis=1)


def kernel(**inputs):
    import concourse.bacc as bacc
    from concourse.bass_utils import run_bass_kernel_spmd

    nc = bacc.Bacc("TRN2", target_bir_lowering=False, num_devices=1, dynamic_dma_scratch_size=64)
    arrays = {name: np.ascontiguousarray(inputs[name]) for name in INPUTS}
    arrays["consts"] = constants()
    args = [nc.dram_tensor(n, a.shape, mybir.dt.from_np(a.dtype), kind="ExternalInput").ap() for n, a in arrays.items()]
    out = nc.dram_tensor("out", arrays["x"].shape, F32, kind="ExternalOutput").ap()
    build(nc, *args, out)
    r = run_bass_kernel_spmd(nc, [arrays], core_ids=[0])
    return r.results[0]["out"]
```
